# Optimizing a Trainium2 kernel written in Bass

```python
import math
import jax, jax.numpy as jnp
from jax import lax
import numpy as np

D_MODEL = 1024
BATCH = 1
SEQ = 1024
DEPTH = 2
DEC_BATCH = 8
DEC_SEQ = 4
PAST_LEN = 1024
PAGE_SIZE = 128

N_MIXERS = 2
N_META = 16
EPS = 1e-6
NEG_INF = -1e30
N_HEADS = 16
HEAD_DIM = D_MODEL // N_HEADS
N_KV_HEADS = 4
GROUP = N_HEADS // N_KV_HEADS
ATT_WIDTH = N_HEADS * HEAD_DIM
KV_WIDTH = N_KV_HEADS * HEAD_DIM
WINDOW = 128
ATT_BLOCK = 128
N_BUCKETS = 32
MAX_DISTANCE = 128
M_PROJ_FACTOR = 2
M_INNER = M_PROJ_FACTOR * D_MODEL
M_HEADS = 4
M_HEAD_DIM = M_INNER // M_HEADS
CONV_WIDTH = 4
MLSTM_CHUNK = 64

kernel_name = 'hybrid_swa_mlstm_meta_decode_step'

def n_layers_of(mixer):
    return len(range(mixer, DEPTH, N_MIXERS))

def rmsnorm(x, w):
    xf = x.astype(jnp.float32)
    y = xf * lax.rsqrt(jnp.mean(xf * xf, axis=-1, keepdims=True) + EPS)
    return (y * w.astype(jnp.float32)).astype(x.dtype)

def rel_bucket(dist):
    n = jnp.maximum(dist, 0)
    max_exact = N_BUCKETS // 2
    nf = jnp.maximum(n, 1).astype(jnp.float32)
    large = max_exact + (jnp.log(nf / max_exact) / math.log(MAX_DISTANCE / max_exact)
                         * (N_BUCKETS - max_exact)).astype(jnp.int32)
    large = jnp.minimum(large, N_BUCKETS - 1)
    return jnp.where(n < max_exact, n, large)

def swa_project(h, w_in, q_norm, k_norm):
    B, T, _ = h.shape
    proj = h @ w_in
    q = proj[..., :ATT_WIDTH].reshape(B, T, N_KV_HEADS, GROUP, HEAD_DIM)
    k = proj[..., ATT_WIDTH:ATT_WIDTH + KV_WIDTH].reshape(B, T, N_KV_HEADS, HEAD_DIM)
    v = proj[..., ATT_WIDTH + KV_WIDTH:ATT_WIDTH + 2 * KV_WIDTH].reshape(B, T, N_KV_HEADS, HEAD_DIM)
    gate = proj[..., ATT_WIDTH + 2 * KV_WIDTH:]
    return rmsnorm(q, q_norm), rmsnorm(k, k_norm), v, gate

def swa_attend(q, k, v, q_pos, k_pos, k_valid, rel_bias, sinks):
    n_blk, t_q = q_pos.shape
    t_k = k_pos.shape[1]
    dist = q_pos[:, :, None] - k_pos[:, None, :]
    mask = k_valid[:, None, :] & (dist >= 0) & ((dist <= WINDOW) | (k_pos[:, None, :] < N_META))
    bias = jnp.transpose(rel_bias.astype(jnp.float32)[rel_bucket(dist)], (0, 3, 1, 2))
    bias = bias.reshape(n_blk, N_KV_HEADS, GROUP, t_q, t_k)
    logits = jnp.einsum('bnqkgd,bnskd->bnkgqs', q, k).astype(jnp.float32) * (HEAD_DIM ** -0.5) + bias[None]
    logits = jnp.where(mask[None, :, None, None], logits, NEG_INF)
    sink = jnp.broadcast_to(sinks.astype(jnp.float32).reshape(1, 1, N_KV_HEADS, GROUP, 1, 1),
                            logits.shape[:-1] + (1,))
    probs = jax.nn.softmax(jnp.concatenate([logits, sink], axis=-1), axis=-1)[..., :-1]
    return jnp.einsum('bnkgqs,bnskd->bnqkgd', probs.astype(v.dtype), v)

def swa_prompt(h, rel_bias, w_in, q_norm, k_norm, sinks, w_out):
    B, T, _ = h.shape
    n_real = T - N_META
    n_blk = n_real // ATT_BLOCK
    q, k, v, gate = swa_project(h, w_in, q_norm, k_norm)
    meta_pos = jnp.arange(N_META, dtype=jnp.int32)
    o_meta = swa_attend(q[:, None, :N_META], k[:, None, :N_META], v[:, None, :N_META],
                        meta_pos[None], meta_pos[None], jnp.ones((1, N_META), bool), rel_bias, sinks)
    qb = q[:, N_META:].reshape(B, n_blk, ATT_BLOCK, N_KV_HEADS, GROUP, HEAD_DIM)

    def band_rows(a):
        cur = a[:, N_META:].reshape(B, n_blk, ATT_BLOCK, N_KV_HEADS, HEAD_DIM)
        prev = jnp.concatenate([jnp.zeros_like(cur[:, :1]), cur[:, :-1]], axis=1)
        meta = jnp.broadcast_to(a[:, None, :N_META], (B, n_blk, N_META, N_KV_HEADS, HEAD_DIM))
        return jnp.concatenate([meta, prev, cur], axis=2)

    blk = jnp.arange(n_blk, dtype=jnp.int32)[:, None]
    q_pos = N_META + blk * ATT_BLOCK + jnp.arange(ATT_BLOCK, dtype=jnp.int32)[None]
    band_pos = N_META + (blk - 1) * ATT_BLOCK + jnp.arange(2 * ATT_BLOCK, dtype=jnp.int32)[None]
    k_pos = jnp.concatenate([jnp.broadcast_to(meta_pos[None], (n_blk, N_META)), band_pos], axis=1)
    k_valid = jnp.concatenate([jnp.ones((n_blk, N_META), bool), band_pos >= N_META], axis=1)
    o_real = swa_attend(qb, band_rows(k), band_rows(v), q_pos, k_pos, k_valid, rel_bias, sinks)
    o = jnp.concatenate([o_meta.reshape(B, N_META, ATT_WIDTH), o_real.reshape(B, n_real, ATT_WIDTH)], axis=1)
    y = (o * jax.nn.silu(gate)) @ w_out
    n_buf = min(WINDOW, T)
    return y, k[:, T - n_buf:], v[:, T - n_buf:], k[:, :N_META], v[:, :N_META]

def swa_sample(h, cache_k, cache_v, meta_k, meta_v, rel_bias, w_in, q_norm, k_norm, sinks, w_out):
    B, T, _ = h.shape
    n_buf = cache_k.shape[1]
    q, k, v, gate = swa_project(h, w_in, q_norm, k_norm)
    win_k = jnp.concatenate([cache_k.astype(k.dtype), k], axis=1)
    win_v = jnp.concatenate([cache_v.astype(v.dtype), v], axis=1)
    keys = jnp.concatenate([meta_k.astype(k.dtype), win_k], axis=1)[:, None]
    vals = jnp.concatenate([meta_v.astype(v.dtype), win_v], axis=1)[:, None]
    buf_pos = PAST_LEN - n_buf + jnp.arange(n_buf, dtype=jnp.int32)
    new_pos = PAST_LEN + jnp.arange(T, dtype=jnp.int32)
    k_pos = jnp.concatenate([jnp.arange(N_META, dtype=jnp.int32), buf_pos, new_pos])[None]
    k_valid = jnp.concatenate([jnp.ones((N_META,), bool), buf_pos >= N_META, jnp.ones((T,), bool)])[None]
    o = swa_attend(q[:, None], keys, vals, new_pos[None], k_pos, k_valid, rel_bias, sinks)
    y = (o.reshape(B, T, ATT_WIDTH) * jax.nn.silu(gate)) @ w_out
    return y, win_k[:, T:], win_v[:, T:]

def mlstm_chunkwise(q, k, v, i_pre, log_f, state, chunk):
    B, T, H, D = q.shape
    n_chunks = T // chunk

    def to_chunks(a):
        return jnp.moveaxis(a.reshape((B, n_chunks, chunk) + a.shape[2:]), 1, 0)

    causal = jnp.tril(jnp.ones((chunk, chunk), bool))

    def step(carry, xs):
        C, n, m = carry
        qc, kc, vc, ic, fc = xs
        b = jnp.cumsum(fc, axis=1)
        g = b[:, -1]
        log_d = b[:, :, None, :] - b[:, None, :, :] + ic[:, None, :, :]
        log_d = jnp.where(causal[None, :, :, None], log_d, -jnp.inf)
        inter = b + m[:, None, :]
        m_t = jnp.maximum(inter, jnp.max(log_d, axis=2))
        w_intra = jnp.exp(log_d - m_t[:, :, None, :])
        w_inter = jnp.exp(inter - m_t)
        s = jnp.einsum('bthd,bjhd->btjh', qc, kc) * w_intra
        num = jnp.einsum('btjh,bjhd->bthd', s, vc) + w_inter[..., None] * jnp.einsum('bthd,bhde->bthe', qc, C)
        den = jnp.sum(s, axis=2) + w_inter * jnp.einsum('bthd,bhd->bth', qc, n)
        h = num / jnp.maximum(jnp.abs(den), jnp.exp(-m_t))[..., None]
        lw = g[:, None, :] - b + ic
        m_new = jnp.maximum(g + m, jnp.max(lw, axis=1))
        wk = jnp.exp(lw - m_new[:, None, :])
        decay = jnp.exp(g + m - m_new)
        C_new = decay[..., None, None] * C + jnp.einsum('bjhd,bjhe->bhde', kc * wk[..., None], vc)
        n_new = decay[..., None] * n + jnp.einsum('bjh,bjhd->bhd', wk, kc)
        return (C_new, n_new, m_new), h

    state, hs = lax.scan(step, state, tuple(to_chunks(a) for a in (q, k, v, i_pre, log_f)))
    return state, jnp.moveaxis(hs, 0, 1).reshape(B, T, H, D)

def mlstm_branch(h, conv_state, cell_state, plan, w_in, conv_w, conv_b, wq, wk, wv,
                 w_gates, b_gates, head_norm, skip, w_out):
    B, T, _ = h.shape
    proj = h @ w_in
    xm, z, o_pre = proj[..., :M_INNER], proj[..., M_INNER:2 * M_INNER], proj[..., 2 * M_INNER:]
    xpad = jnp.concatenate([conv_state.astype(xm.dtype), xm], axis=1)
    xc = jax.nn.silu(sum(xpad[:, w:w + T] * conv_w[w] for w in range(CONV_WIDTH)) + conv_b)
    xc_h = xc.reshape(B, T, M_HEADS, M_HEAD_DIM)
    q = jnp.einsum('bthd,hde->bthe', xc_h, wq)
    k = jnp.einsum('bthd,hde->bthe', xc_h, wk) * (M_HEAD_DIM ** -0.5)
    v = jnp.einsum('bthd,hde->bthe', xm.reshape(B, T, M_HEADS, M_HEAD_DIM), wv)
    gates = (q.reshape(B, T, M_INNER) @ w_gates[:M_INNER]
             + k.reshape(B, T, M_INNER) @ w_gates[M_INNER:2 * M_INNER]
             + v.reshape(B, T, M_INNER) @ w_gates[2 * M_INNER:] + b_gates).astype(jnp.float32)
    i_pre = gates[..., :M_HEADS]
    log_f = jax.nn.log_sigmoid(gates[..., M_HEADS:])
    qf, kf, vf = (a.astype(jnp.float32) for a in (q, k, v))
    state = tuple(s.astype(jnp.float32) for s in cell_state)
    outs, start = [], 0
    for seg_len, chunk in plan:
        seg = slice(start, start + seg_len)
        state, h_seg = mlstm_chunkwise(qf[:, seg], kf[:, seg], vf[:, seg], i_pre[:, seg], log_f[:, seg], state, chunk)
        outs.append(h_seg)
        start += seg_len
    h_cell = jnp.concatenate(outs, axis=1)
    mu = jnp.mean(h_cell, axis=-1, keepdims=True)
    var = jnp.mean(jnp.square(h_cell - mu), axis=-1, keepdims=True)
    h_norm = ((h_cell - mu) * lax.rsqrt(var + EPS)).reshape(B, T, M_INNER) * head_norm.astype(jnp.float32)
    h_out = (jax.nn.sigmoid(o_pre.astype(jnp.float32)) * h_norm).astype(h.dtype)
    y = ((h_out + skip * xc) * jax.nn.silu(z)) @ w_out
    return y, (state[0], state[1], state[2], xpad[:, T:])

def setup_inputs(seed: int = 0) -> dict:
    key = jax.random.key(seed)
    keys = iter(jax.random.split(key, 64))

    def rnd(shape, scale):
        return scale * jax.random.normal(next(keys), shape, jnp.float32)

    n_swa, n_ml = n_layers_of(0), n_layers_of(1)
    n_buf = min(WINDOW, PAST_LEN)
    in_width = 2 * ATT_WIDTH + 2 * KV_WIDTH
    f_bias = jnp.linspace(3.0, 6.0, M_HEADS, dtype=jnp.float32)[None] + rnd((n_ml, M_HEADS), 0.1)
    return {
        'x_prompt': rnd((BATCH, SEQ, D_MODEL), 1.0),
        'x_sample': rnd((DEC_BATCH, DEC_SEQ, D_MODEL), 1.0),
        'cache_swa_k': rnd((n_swa, DEC_BATCH, n_buf, N_KV_HEADS, HEAD_DIM), 1.0),
        'cache_swa_v': rnd((n_swa, DEC_BATCH, n_buf, N_KV_HEADS, HEAD_DIM), 1.0),
        'cache_swa_meta_k': rnd((n_swa, DEC_BATCH, N_META, N_KV_HEADS, HEAD_DIM), 1.0),
        'cache_swa_meta_v': rnd((n_swa, DEC_BATCH, N_META, N_KV_HEADS, HEAD_DIM), 1.0),
        'state_mlstm_c': rnd((n_ml, DEC_BATCH, M_HEADS, M_HEAD_DIM, M_HEAD_DIM), 0.02),
        'state_mlstm_n': rnd((n_ml, DEC_BATCH, M_HEADS, M_HEAD_DIM), 0.02),
        'state_mlstm_m': rnd((n_ml, DEC_BATCH, M_HEADS), 1.0),
        'state_mlstm_conv': rnd((n_ml, DEC_BATCH, CONV_WIDTH - 1, M_INNER), 1.0),
        'meta_tokens': rnd((N_META, D_MODEL), 1.0),
        'rel_bias': rnd((N_BUCKETS, N_HEADS), 0.5),
        'norm_w': 1.0 + rnd((DEPTH, D_MODEL), 0.02),
        'swa_w_in': rnd((n_swa, D_MODEL, in_width), D_MODEL ** -0.5),
        'swa_q_norm': 1.0 + rnd((n_swa, HEAD_DIM), 0.02),
        'swa_k_norm': 1.0 + rnd((n_swa, HEAD_DIM), 0.02),
        'swa_sinks': rnd((n_swa, N_HEADS), 0.5),
        'swa_w_out': rnd((n_swa, ATT_WIDTH, D_MODEL), ATT_WIDTH ** -0.5),
        'mlstm_w_in': rnd((n_ml, D_MODEL, 3 * M_INNER), D_MODEL ** -0.5),
        'mlstm_conv_w': rnd((n_ml, CONV_WIDTH, M_INNER), CONV_WIDTH ** -0.5),
        'mlstm_conv_b': rnd((n_ml, M_INNER), 0.02),
        'mlstm_wq': rnd((n_ml, M_HEADS, M_HEAD_DIM, M_HEAD_DIM), M_HEAD_DIM ** -0.5),
        'mlstm_wk': rnd((n_ml, M_HEADS, M_HEAD_DIM, M_HEAD_DIM), M_HEAD_DIM ** -0.5),
        'mlstm_wv': rnd((n_ml, M_HEADS, M_HEAD_DIM, M_HEAD_DIM), M_HEAD_DIM ** -0.5),
        'mlstm_w_gates': rnd((n_ml, 3 * M_INNER, 2 * M_HEADS), (3 * M_INNER) ** -0.5),
        'mlstm_b_gates': jnp.concatenate([rnd((n_ml, M_HEADS), 0.1), f_bias], axis=-1),
        'mlstm_head_norm': 1.0 + rnd((n_ml, M_INNER), 0.02),
        'mlstm_skip': 1.0 + rnd((n_ml, M_INNER), 0.02),
        'mlstm_w_out': rnd((n_ml, M_INNER, D_MODEL), M_INNER ** -0.5),
    }

def stack_rows(rows, idx):
    return jnp.stack([r[idx] for r in rows])

def reference(x_prompt, x_sample, cache_swa_k, cache_swa_v, cache_swa_meta_k, cache_swa_meta_v,
              state_mlstm_c, state_mlstm_n, state_mlstm_m, state_mlstm_conv,
              meta_tokens, rel_bias, norm_w, swa_w_in, swa_q_norm, swa_k_norm, swa_sinks, swa_w_out,
              mlstm_w_in, mlstm_conv_w, mlstm_conv_b, mlstm_wq, mlstm_wk, mlstm_wv,
              mlstm_w_gates, mlstm_b_gates, mlstm_head_norm, mlstm_skip, mlstm_w_out):
    B, n_real, _ = x_prompt.shape
    meta = jnp.broadcast_to(meta_tokens.astype(x_prompt.dtype)[None], (B, N_META, D_MODEL))
    xp = jnp.concatenate([meta, x_prompt], axis=1)
    xs = x_sample
    prompt_plan = ((N_META, N_META), (n_real, MLSTM_CHUNK))
    sample_plan = ((x_sample.shape[1], x_sample.shape[1]),)
    swa_p, swa_s, ml_p, ml_s = [], [], [], []
    for layer in range(DEPTH):
        j = layer // N_MIXERS
        hp = rmsnorm(xp, norm_w[layer])
        hs = rmsnorm(xs, norm_w[layer])
        if layer % N_MIXERS == 0:
            aw = (swa_w_in[j], swa_q_norm[j], swa_k_norm[j], swa_sinks[j], swa_w_out[j])
            yp, *p_rows = swa_prompt(hp, rel_bias, *aw)
            ys, *s_rows = swa_sample(hs, cache_swa_k[j], cache_swa_v[j], cache_swa_meta_k[j],
                                     cache_swa_meta_v[j], rel_bias, *aw)
            swa_p.append(p_rows)
            swa_s.append(s_rows)
        else:
            mw = (mlstm_w_in[j], mlstm_conv_w[j], mlstm_conv_b[j], mlstm_wq[j], mlstm_wk[j], mlstm_wv[j],
                  mlstm_w_gates[j], mlstm_b_gates[j], mlstm_head_norm[j], mlstm_skip[j], mlstm_w_out[j])
            zero_cell = (jnp.zeros((B, M_HEADS, M_HEAD_DIM, M_HEAD_DIM), jnp.float32),
                         jnp.zeros((B, M_HEADS, M_HEAD_DIM), jnp.float32),
                         jnp.zeros((B, M_HEADS), jnp.float32))
            zero_conv = jnp.zeros((B, CONV_WIDTH - 1, M_INNER), xp.dtype)
            yp, p_rows = mlstm_branch(hp, zero_conv, zero_cell, prompt_plan, *mw)
            ys, s_rows = mlstm_branch(hs, state_mlstm_conv[j],
                                      (state_mlstm_c[j], state_mlstm_n[j], state_mlstm_m[j]), sample_plan, *mw)
            ml_p.append(p_rows)
            ml_s.append(s_rows)
        xp = xp + yp
        xs = xs + ys
    sd = state_mlstm_c.dtype
    return (xp[:, N_META:], xs,
            stack_rows(swa_p, 0), stack_rows(swa_p, 1), stack_rows(swa_p, 2), stack_rows(swa_p, 3),
            stack_rows(ml_p, 0).astype(sd), stack_rows(ml_p, 1).astype(sd), stack_rows(ml_p, 2).astype(sd),
            stack_rows(ml_p, 3),
            stack_rows(swa_s, 0), stack_rows(swa_s, 1),
            stack_rows(ml_s, 0).astype(sd), stack_rows(ml_s, 1).astype(sd), stack_rows(ml_s, 2).astype(sd),
            stack_rows(ml_s, 3))


_drawn_inputs = setup_inputs


def setup_inputs(seed=0):
    import zlib

    import numpy as np

    out = dict(_drawn_inputs(seed))
    spreads = {}
    factors = {'swa_q_norm': 8.0, 'swa_sinks': 52.514, 'mlstm_head_norm': 34.432, 'mlstm_skip': 28.274}
    for name, (base, spread) in spreads.items():
        noise = np.random.default_rng([zlib.crc32(name.encode()), seed]).standard_normal(out[name].shape)
        drawn = base * np.exp(spread * noise) if base else spread * noise
        out[name] = __import__('jax').numpy.asarray(drawn.astype(out[name].dtype))
    for name, factor in factors.items():
        out[name] = (out[name] * factor).astype(out[name].dtype)
    return out
```

```python
import numpy as np

import concourse.bass as bass
from concourse import mybir

F32 = mybir.dt.float32
F32R = mybir.dt.float32r
ALU = mybir.AluOpType
ACT = mybir.ActivationFunctionType
AX = mybir.AxisListType

D = 1024
SEQ = 1024
DECB = 8
DECT = 4
META = 16
NH = 16
HD = 64
KVH = 4
WIN = 128
NBK = 32
INNER = 2048
MH = 4
MD = 512
CW = 4
EPS = 1e-6
NEG = -1e30
P = 128
NPR = META + SEQ
NSM = DECB * DECT
T = NPR + NSM
GRP = 360
TP = 3 * GRP
KT = D // P
NBLK = SEQ // WIN
RBAND = 384
RMETA = 144
RROW = RBAND + RMETA + META
KEYS = META + 2 * WIN
SKEYS = META + WIN + DECT
ICOL = 1 + NPR + DECB * (DECT + 1)


class Idx:

    def __init__(self, a, g=0, U=0):
        self.a, self.g, self.U = a, g, U

    @property
    def v(self):
        return self.a + self.g * self.U if self.U else self.a

    def __add__(self, k):
        return Idx(self.a + k, self.g, self.U)

    def div(self, k):
        assert self.U % k == 0
        return self.a // k + self.g * (self.U // k) if self.U else self.a // k

    def mod(self, k):
        assert self.U % k == 0
        return self.a % k


def sweep(eng, start, n, U, step, peel=1, tail=0):
    turns = n // U
    end = turns - tail
    for j in range(peel * U):
        step(Idx(start + j))
    if end - peel > 1:
        with eng.Fori(peel, end) as g:
            for u in range(U):
                step(Idx(start + u, g, U))
    else:
        end = peel
    for j in range(end * U, n):
        step(Idx(start + j))


def due(n):
    n = n.v if isinstance(n, Idx) else n
    return max(n, 0) if isinstance(n, int) else n


def wait_apart(eng, sem, n):
    n = n.v if isinstance(n, Idx) else n
    if not isinstance(n, int):
        n = eng.to_reg(n)
        eng.wait_ge(sem, 1)
    eng.wait_ge(sem, due(n))


def diagonal_onehot():
    def bucket(d):
        d = np.maximum(d, 0)
        nf = np.maximum(d, 1).astype(np.float32)
        large = 16 + (np.log(nf / np.float32(16)) / np.float32(np.log(8.0)) * 16).astype(np.int32)
        return np.where(d < 16, d, np.minimum(large, NBK - 1))
    oh = np.zeros((NBK + 1, RROW), np.float32)
    u = np.arange(RBAND)
    dist = 255 - u
    seen = (dist >= 0) & (dist <= WIN)
    oh[bucket(dist)[seen], u[seen]] = 1.0
    oh[NBK, u[~seen]] = 1.0
    v = np.arange(RMETA)
    oh[bucket(143 - v), RBAND + v] = 1.0
    oh[NBK - 1, RBAND + RMETA:] = 1.0
    return oh


def build(nc, a, o):
    sems = {}
    sem_suffix = ['']

    def sem(name):
        if name not in sems:
            sems[name] = nc.alloc_semaphore(name + sem_suffix[0])
        return sems[name]

    BASE = 1152

    def sb(name, shape, off, dt=F32):
        assert BASE + off + 4 * int(np.prod(shape[1:])) <= 229368, name
        return nc.alloc_sbuf_tensor_at("sb_" + name, shape, dt, offset=BASE + off)

    def scratch(name, shape):
        return nc.dram_tensor("scratch_" + name, shape, F32, kind="Internal").ap()

    def dram(ap, offset, pattern):
        return bass.AP(tensor=ap.tensor, offset=offset, ap=pattern)

    cur = [0]

    def const(name, shape):
        n = 4 * int(np.prod(shape[1:]))
        t = sb(name, shape, cur[0])
        cur[0] += -(-n // 32) * 32
        return t

    ident = const("ident", [P, P])
    ones = const("ones", [P, P])
    headsum = const("headsum", [P, P])
    epsc = const("epsc", [P, 1])
    vrow = const("vrow", [P, P])
    vcol = const("vcol", [P, P])
    nrow = const("nrow", [2, P])
    qkw = const("qkw", [P, 2])
    normw = vcol[:, 0:16].rearrange("p (l k) -> p l k", l=2)
    hvec = const("hvec", [P, 7, 4])
    convw_h = hvec[:, 0:4, :]
    convb_h, hnorm_h, skip_h = hvec[:, 4, :], hvec[:, 5, :], hvec[:, 6, :]
    relb = const("relb", [NBK + 1, NH])
    onehot_at = cur[0]
    onehot = const("onehot", [NBK + 1, RROW])
    rtab = const("rtab", [NH, RROW])
    sinkc = const("sinkc", [NH, 1])
    sinkv = const("sinkv", [P, 1])
    headsel = const("headsel", [NH, P])
    assert cur[0] <= 10240
    WB = 10240
    NSLOT = 3
    SLOT = KT * P * 4
    wraw = [sb(f"wraw{i}", [P, KT * P], WB + i * SLOT) for i in range(NSLOT)]
    whi = [sb(f"whi{i}", [P, KT * P], WB + (NSLOT + i) * SLOT, F32R) for i in range(NSLOT)]
    wlo = [sb(f"wlo{i}", [P, KT * P], WB + (2 * NSLOT + i) * SLOT, F32R) for i in range(NSLOT)]
    BIG = WB + 3 * NSLOT * SLOT
    TB = -(-4 * TP // 32) * 32

    def tiles(name, n, first, dt=F32):
        return sb(name, [P, n, TP], BIG + first * TB, dt)

    hh, hl = tiles("hh", KT, 0, F32R), tiles("hl", KT, KT, F32R)
    kqv = tiles("kqv", 12, 16)
    gate = tiles("gate", KT, 28)
    xT = tiles("xT", KT, 16)
    M0 = BIG + 28 * TB
    xtok = [sb(f"xtok{i}", [P, D], M0 + i * 4 * D) for i in range(3)]
    sq = [tiles(f"sq{i}", 1, 36 + i) for i in range(2)]
    rb = [tiles(f"rb{i}", 1, 38 + i) for i in range(2)]
    hf = [tiles("hf0", 1, 40), tiles("hf1", 1, 34)]

    at = [BIG]

    def abuf(name, shape):
        t = sb(name, shape, at[0])
        at[0] += -(-4 * int(np.prod(shape[1:])) // 32) * 32
        assert at[0] <= BIG + 16 * TB
        return t

    bias = abuf("bias", [P, NH, KEYS])
    V0 = BIG + 26 * TB
    prob = [abuf(f"prob{i}", [P, 4, KEYS]) for i in range(3)] + [sb("prob3", [P, 4, KEYS], V0)]
    probm = [abuf(f"probm{i}", [P, 64]) for i in range(2)]
    probT = [abuf(f"probT{i}", [P, 8 * P]) for i in range(2)]
    probTm = [abuf(f"probTm{i}", [64, P]) for i in range(2)]
    ob = [sb(f"ob{i}", [P, 256], V0 + 4352 + 1024 * i) for i in range(2)]
    og = [sb(f"og{i}", [P, 2, P], V0 + 4352 + 2048 + 1024 * i) for i in range(2)]
    qb = [abuf(f"qb{i}", [P, 8, P]) for i in range(2)]
    kb = [abuf(f"kb{i}", [P, 2, 2, P + META]) for i in range(2)]
    vtok = abuf("vtok", [P, NBLK + 2, 256])
    vbd = abuf("vbd", [64, KVH, 256])
    S0 = [BIG + 36 * TB]

    def sbuf2(name, shape):
        t = sb(name, shape, S0[0])
        S0[0] += -(-4 * int(np.prod(shape[1:])) // 32) * 32
        return t

    ktok = sbuf2("ktok", [P, 3, 256])
    sinkb = sbuf2("sinkb", [P, NH])
    nsink = sbuf2("nsink", [P, NH])
    sinks = sbuf2("sinks", [P, 2])
    stat = sbuf2("stat", [P, 4, 6, 4])
    kc = [sbuf2(f"kc{i}", [P, 256]) for i in range(2)]
    vc = [sbuf2(f"vc{i}", [P, 256]) for i in range(2)]
    kmt = [sbuf2(f"kmt{i}", [META, 256]) for i in range(2)]
    vmt = [sbuf2(f"vmt{i}", [META, 256]) for i in range(2)]
    vnt = [sbuf2(f"vnt{i}", [DECT, 256]) for i in range(2)]
    qsb = [sbuf2(f"qsb{i}", [64, KVH, 32]) for i in range(2)]
    ktb = [sbuf2(f"ktb{i}", [64, KVH, SKEYS]) for i in range(2)]
    biasS = sbuf2("biasS", [P, SKEYS])
    probS = [sb(f"probS{i}", [P, SKEYS], BIG + 26624 + 640 * i) for i in range(2)]
    pts = [sb(f"pts{i}", [P, 3, P], BIG + 26624 + 1280 + 1536 * i) for i in range(2)]
    sstat = sbuf2("sstat", [P, 2, 6])
    obS = [sbuf2(f"obS{i}", [P, 64]) for i in range(2)]
    ogS = sbuf2("ogS", [P, KT, NSM])
    probM = sb("probM", [META, NH, META], BIG + 17408)
    assert S0[0] <= 229368 - BASE

    probMT = sb("probMT", [META, NH, META], BIG + 17408 + 4352)
    oh = tiles("oh", KT, 28, F32R)
    ol = tiles("ol", KT, 18, F32R)

    x1T = tiles("x1T", KT, 0)
    xres = [tiles(f"xres{i}", 1, 16 + i) for i in range(2)]
    h1h, h1l = tiles("h1h", KT, 16, F32R), tiles("h1l", KT, 24, F32R)
    xmh, xml = tiles("xmh", 4, 0, F32R), tiles("xml", 4, 4, F32R)
    xch, xcl = tiles("xch", 4, 8, F32R), tiles("xcl", 4, 12, F32R)
    sz = [tiles(f"sz{i}", 1, 32 + i) for i in range(2)]
    st = [tiles(f"st{i}", 1, 34 + i) for i in range(3)]
    xc = [tiles(f"xc{i}", 1, 37 + i) for i in range(2)]
    X0 = BIG + 39 * TB
    XPR = CW - 1 + NPR
    xr = [sb(f"xr{i}", [P, XPR + DECB * (CW - 1 + DECT) + 1], X0 + 4416 * i) for i in range(2)]
    wg = sb("wg", [P, 12, 36], X0 + 2 * 4416)
    cstate = sb("cstate", [P, 16, DECB * (CW - 1)], onehot_at)
    ctail = sb("ctail", [P, 16, 27], onehot_at + 1536)
    crow = sb("crow", [DECB * (CW - 1), INNER], BIG + 31 * TB)
    orow = sb("orow", [27, INNER], BIG + 8 * TB)
    uh, ul = tiles("uh", 4, 8, F32R), tiles("ul", 4, 12, F32R)
    R0 = [BIG + 16 * TB]

    def rbuf(name, shape, dt=F32):
        t = sb(name, shape, R0[0], dt)
        R0[0] += -(-4 * int(np.prod(shape[1:])) // 32) * 32
        return t

    NCH = NBLK + 2
    col = rbuf("col", [P, NCH, P])
    bcs = rbuf("bcs", [P, 2, MH, 17])
    wsb = rbuf("wsb", [P, MH, NSM])
    absm = rbuf("absm", [NSM, MH, NSM])
    hcol = rbuf("hcol", [P, NCH, 3])
    hbc = rbuf("hbc", [P, 2, 17])
    hws = rbuf("hws", [P, NSM])
    habs = rbuf("habs", [NSM, NSM])
    tri = rbuf("tri", [P, P])
    trism = rbuf("trism", [NSM, NSM])
    blkm = rbuf("blkm", [NSM, DECB])
    brow = rbuf("brow", [P, 1])
    scal = rbuf("scal", [MH, 5, 17])
    wrow = rbuf("wrow", [MH, NSM])
    rss = rbuf("rss", [P, NSM])
    snin = rbuf("snin", [DECB * MH, MD])
    sn = rbuf("sn", [P, 4, DECB * MH])
    snew = rbuf("snew", [P, 4, DECB * MH])
    nall = rbuf("nall", [P, MH, 4])
    nrow4 = rbuf("nrow4", [4 * MH, P])
    chin = [rbuf(f"chin{i}", [P, 5, 4, P]) for i in range(3)]
    smin = rbuf("smin", [P, 5, 4, NSM])
    ROWS = R0[0]
    rown = [sb(f"row{i}", [P if i == 6 else MH, ICOL], ROWS + 4352 * i) for i in range(7)]
    gi, lf, cb, mm_, msk, fx, rs = rown
    cst = rbuf("cst", [P, 4, MD])
    nst = rbuf("nst", [P, 4])
    scs = [rbuf(f"scs{i}", [P, 4, MD]) for i in range(2)]
    abc = rbuf("abc", [P, NPR])
    ee = [rbuf(f"ee{i}", [P, P]) for i in range(2)]
    swb = [rbuf(f"swb{i}", [P, P]) for i in range(2)]
    wnt = [rbuf(f"wnt{i}", [P, P]) for i in range(2)]
    kw = [rbuf(f"kw{i}", [P, MD]) for i in range(2)]
    vt = [rbuf(f"vt{i}", [P, MD]) for i in range(2)]
    qs = [rbuf(f"qs{i}", [P, 4, P]) for i in range(2)]
    ees, sws = rbuf("ees", [NSM, NSM]), rbuf("sws", [NSM, NSM])
    kws, vts = rbuf("kws", [NSM, MD]), rbuf("vts", [NSM, MD])
    qss, prod = rbuf("qss", [P, 4, NSM]), rbuf("prod", [P, 4, NSM])
    kwz = [rbuf(f"kwz{i}", [NSM, MD]) for i in range(2)]
    nums = rbuf("nums", [NSM, MD])
    ntmp = rbuf("ntmp", [P, 4, DECB])
    hb = [rbuf(f"hb{i}", [P, MD]) for i in range(2)]
    ub = [rbuf(f"ub{i}", [P, 4, P]) for i in range(2)]
    cs = rbuf("cs", [P, 2, 16])
    ytok = [sb(f"ytok{i}", [P, D], ROWS + 4096 * i) for i in range(2)]

    ps = [nc.alloc_psum_tensor(f"ps{i}", [P, 3, 512], F32) for i in range(2)]
    pm = [nc.alloc_psum_tensor(f"pm{i}", [P, 512], F32) for i in range(2)]

    xT_d = scratch("xT", [KT, P, TP])
    x1T_d = scratch("x1T", [KT, P, TP])
    vnew_d = scratch("vnew", [DECB, DECT, 256])
    q_d, k_d, v_d = (scratch(n, [MH * 4, P, TP]) for n in "qkv")
    ga_d, gb_d = scratch("ga", [MH * 4, P, TP]), scratch("gb", [MH * 4, P, TP])
    arow_d, srow_d, wrow_d = scratch("arow", [MH, ICOL]), scratch("srow", [2, MH, 17]), scratch("wrow", [MH, NSM])
    HREL = P * (RROW + 1)
    rel_d = scratch("rel", [NH * HREL])
    knew_d = scratch("knew", [DECB, DECT, 256])

    def slot_load(eng, n, src, k):
        wait_apart(eng, sem("w_lo"), n + (1 - NSLOT))
        eng.dma_start(wraw[n.mod(NSLOT)][:, :].rearrange("p (k c) -> p k c", k=k), src)\
            .then_inc(sem(f"w_loaded{n.mod(NSLOT)}"), 16)

    def split_hi(act, n, used):
        q = n.mod(NSLOT)
        act.wait_ge(sem(f"w_loaded{q}"), due(16 * n.div(NSLOT) + 16))
        act.wait_ge(sem("ps_full"), due(used))
        act.activation(whi[q][:, :], wraw[q][:, :], ACT.Copy).then_inc(sem("w_hi"), 1)

    def split_lo(dve, n):
        q = n.mod(NSLOT)
        dve.wait_ge(sem("w_hi"), due(n + 1))
        dve.tensor_tensor(wlo[q][:, :], wraw[q][:, :], whi[q][:, :].bitcast(F32), ALU.subtract)\
            .then_inc(sem("w_lo"), 1)

    def product(pe, n, mt, k, c, ah, al, mid=None, made=None):
        q, s = n.mod(NSLOT), mt.mod(2)
        pe.wait_ge(sem("w_lo"), due(n + 1))
        pe.wait_ge(sem(f"ps_free{s}"), due(mt.div(2)))
        H = whi[q][:, :].rearrange("p (k m) -> p k m", k=k)
        L = wlo[q][:, :].rearrange("p (k m) -> p k m", k=k)
        for kk in range(k):
            if made is not None:
                pe.wait_ge(sem("rms_lo"), made + kk + 1)
            for i, (w, x) in enumerate(((H, ah), (H, al), (L, ah))):
                for g in range(3):
                    last = pe.matmul(ps[s][:, g, 0:GRP], w[:, kk, c * P:(c + 1) * P],
                                     x[:, kk, g * GRP:(g + 1) * GRP],
                                     start=(kk == 0 and i == 0), stop=(kk == k - 1 and i == 2))
            if mid is not None and kk == k // 2:
                mid()
        last.then_inc(sem("ps_full"), 1)

    def v3(t):
        return t.rearrange("p (g c) -> p g c", g=3)

    def rms_act(act, src, oh, c0, ready):
        for k in range(KT):
            act.wait_ge(ready[0], due(ready[1](k)))
            act.wait_ge(sem("rms_mm"), due(c0 * KT + k - 1))
            act.activation(sq[k % 2][:, 0, :], src[:, k, :], ACT.Square).then_inc(sem("rms_sq"), 1)
        act.wait_ge(sem("rms_mm"), due(c0 * KT + KT))
        act.activation(v3(rb[1][:, 0, :]), ps[0][:, :, 0:GRP], ACT.Ln, bias=epsc[:, 0:1], scale=1.0 / D)\
            .then_inc(sem("rms_root"), 1)
        act.wait_ge(sem("rms_root"), due(c0 + 1))
        act.activation(rb[1][:, 0, :], rb[1][:, 0, :], ACT.Exp, scale=-0.5).then_inc(sem("rms_rec"), 1)
        for k in range(KT):
            act.wait_ge(sem("rms_hf"), due(c0 * KT + k + 1))
            act.activation(oh[:, k, :], hf[k % 2][:, 0, :], ACT.Copy).then_inc(sem("rms_hi"), 1)

    def rms_pe(pe, c0):
        for k in range(KT):
            pe.wait_ge(sem("rms_sq"), due(c0 * KT + k + 1))
            for g in range(3):
                last = pe.matmul(ps[0][:, g, 0:GRP], ones[:, :], sq[k % 2][:, 0, g * GRP:(g + 1) * GRP],
                                 start=(k == 0), stop=(k == KT - 1))
            last.then_inc(sem("rms_mm"), 1)

    def rms_dve(dve, src, oh, ol, c0, w):
        dve.wait_ge(sem("rms_rec"), due(c0 + 1))
        for k in range(KT + 1):
            if k < KT:
                dve.wait_ge(sem("rms_lo"), due(c0 * KT + k - 1))
                dve.scalar_tensor_tensor(hf[k % 2][:, 0, :], src[:, k, :], normw[:, w, k:k + 1], rb[1][:, 0, :],
                                         ALU.mult, ALU.mult).then_inc(sem("rms_hf"), 1)
            if k > 0:
                dve.wait_ge(sem("rms_hi"), due(c0 * KT + k))
                dve.tensor_tensor(ol[:, k - 1, :], hf[(k - 1) % 2][:, 0, :], oh[:, k - 1, :].bitcast(F32),
                                  ALU.subtract).then_inc(sem("rms_lo"), 1)

    def hn_square(act, m):
        act.wait_ge(sem(f"ps_free{m.mod(2)}"), due(m.div(2) + 1))
        n = 3 * m.a - 3 + 3 * m.g * m.U if m.U else 3 * m.a - 3
        act.wait_ge(sem("hn_grp"), due(n))
        act.activation(sq[m.mod(2)][:, 0, :], kqv[:, bass.ds(m.v, 1), :].rearrange("p a c -> p (a c)"), ACT.Square)\
            .then_inc(sem("hn_sq"), 1)

    def hn_pe(pe, m, g):
        if g == 0:
            pe.wait_ge(sem("hn_sq"), due(m + 1))
        seq = 3 * m.v + g
        pe.wait_ge(sem("hn_ln"), due(seq - 1))
        pe.matmul(pm[(3 * m.mod(2) + g) % 2][:, 0:GRP], headsum[:, :],
                  sq[m.mod(2)][:, 0, g * GRP:(g + 1) * GRP], start=True, stop=True)\
            .then_inc(sem("hn_grp"), 1)

    def hn_act(act, m):
        r = rb[m.mod(2)]
        act.wait_ge(sem("hn_done"), due(m + (-1)))
        for g in range(3):
            act.wait_ge(sem("hn_grp"), due(3 * m.v + g + 1))
            act.activation(r[:, 0, g * GRP:(g + 1) * GRP], pm[(3 * m.mod(2) + g) % 2][:, 0:GRP], ACT.Ln,
                           bias=epsc[:, 0:1], scale=1.0 / HD).then_inc(sem("hn_ln"), 1)
        act.wait_ge(sem("hn_ln"), due(3 * m.v + 3))
        act.activation(r[:, 0, :], r[:, 0, :], ACT.Exp, scale=-0.5).then_inc(sem("hn_rs"), 1)

    def hn_dve(dve, m):
        dve.wait_ge(sem("hn_rs"), due(m + 1))
        t = kqv[:, m.v, :]
        dve.scalar_tensor_tensor(t, t, qkw[:, (0 if m.v < 2 else 1):(1 if m.v < 2 else 2)], rb[m.mod(2)][:, 0, :],
                                 ALU.mult, ALU.mult).then_inc(sem("hn_done"), 1)

    S_BANK = [ps[0][:, 0, :], ps[0][:, 1, :], ps[1][:, 0, :], ps[1][:, 1, :]]
    T_BANK = [ps[0][:, 2, :], ps[1][:, 2, :]]
    UNITS = NBLK * KVH

    def att_scores(pe, s):
        kv, b = s.mod(4), s.mod(8) // 4
        if kv == 0:
            pe.wait_ge(sem(f"blk{b}"), due(64 * s.div(8) + 64))
        pe.wait_ge(sem("s_read"), due(s))
        for g in range(4):
            H = 4 * kv + g
            f, r = H % 2, slice(64 * (H % 2), 64 * (H % 2) + 64)
            w = qb[b][r, H // 2, :]
            turned = 0 if kv % 2 == f else 1
            pe.matmul(S_BANK[g][:, 0:P], w, kb[1 - b][r, kv // 2, turned, 0:P], start=True, stop=True)
            last = pe.matmul(S_BANK[g][:, P:KEYS], w, kb[b][r, kv // 2, turned, :], start=True, stop=True)
        last.then_inc(sem("s_ready"), 1)

    def att_softmax_dve(dve, s):
        kv, q = s.mod(4), s.mod(4)
        H = slice(4 * kv, 4 * kv + 4)
        dve.wait_ge(sem("s_ready"), due(s + 1))
        dve.wait_ge(sem("pt_ready"), due(s + (-3)))
        for j in range(2):
            last = dve.scalar_tensor_tensor(prob[q][:, 2 * j:2 * j + 2, :], ps[j][:, 0:2, 0:KEYS], HD ** -0.5,
                                            bias[:, 4 * kv + 2 * j:4 * kv + 2 * j + 2, :], ALU.mult, ALU.add)
            last.then_inc(sem("biased"), 1)
        dve.wait_ge(sem("biased"), due(2 * s.v + 2))
        dve.sem_inc(sem("s_read"), 1)
        dve.wait_ge(sem("den"), due(s + (-3)))
        dve.tensor_reduce(stat[:, q, 0, :], prob[q][:, :, :], AX.X, ALU.max).then_inc(sem("smax"), 1)
        dve.wait_ge(sem("smax"), due(s + 1))
        dve.scalar_tensor_tensor(stat[:, q, 1, :], stat[:, q, 0, :], -1.0, nsink[:, H], ALU.mult, ALU.min)\
            .then_inc(sem("nmax"), 1)
        dve.wait_ge(sem("nmax"), due(s + 1))
        dve.tensor_tensor(stat[:, q, 3, :], stat[:, q, 1, :], sinkb[:, H], ALU.add).then_inc(sem("a_done"), 1)

    def att_exp(act, s):
        q = s.mod(4)
        act.wait_ge(sem("a_done"), due(s + 1))
        for g in range(4):
            act.activation(prob[q][:, g, :], prob[q][:, g, :], ACT.Exp, bias=stat[:, q, 1, g:g + 1],
                           accum_out=stat[:, q, 2, g:g + 1])
        act.activation(stat[:, q, 3, :], stat[:, q, 3, :], ACT.Exp).then_inc(sem("e_done"), 1)

    def att_turn(pe, s):
        q = s.mod(2)
        pe.wait_ge(sem("e_done"), due(s + 1))
        pe.wait_ge(sem("pta"), due(s))
        pe.wait_ge(sem("ptb"), due(s))
        pe.wait_ge(sem("gated"), due(s + (-1)))
        for g in range(4):
            for c in range(2):
                pe.transpose(T_BANK[g // 2][:, (g % 2) * 256 + c * P:(g % 2) * 256 + c * P + P],
                             prob[s.mod(4)][:, g, c * P:(c + 1) * P], ident[:, :])
        wait_apart(pe, sem("packed"), s + 1)
        pe.transpose(pm[q][0:64, 256:384], probm[q][:, :], ident[:, :]).then_inc(sem("pt_ready"), 1)

    def att_pack(gp, s):
        q = s.mod(2)
        wait_apart(gp, sem("e_done"), s + 1)
        wait_apart(gp, sem("pt_ready"), s + (-1))
        gp.tensor_copy(probm[q][:, :].rearrange("p (g k) -> p g k", g=4), prob[s.mod(4)][:, :, 2 * P:KEYS]).then_inc(sem("packed"), 1)

    def att_turned_act(act, s):
        q = s.mod(2)
        act.wait_ge(sem("pt_ready"), due(s + 1))
        act.wait_ge(sem("pv_done"), due(s + (-1)))
        act.activation(probTm[q][:, :], pm[q][0:64, 256:384], ACT.Copy)
        act.activation(probT[q][:, 0:512], T_BANK[0], ACT.Copy).then_inc(sem("pta"), 1)

    def att_turned_dve(dve, s):
        q = s.mod(2)
        dve.wait_ge(sem("pt_ready"), due(s + 1))
        dve.wait_ge(sem("pv_done"), due(s + (-1)))
        dve.tensor_copy(probT[q][:, 512:1024], T_BANK[1]).then_inc(sem("ptb"), 1)

    def att_values(pe, s):
        kv, q, blk = s.mod(4), s.mod(2), s.div(4)
        pe.wait_ge(sem("pta"), due(s + 1))
        pe.wait_ge(sem("ptb"), due(s + 1))
        pe.matmul(pm[q][:, 0:256], probTm[q][:, :], vbd[:, kv, :], start=True, stop=False, skip_group_check=True)
        for g in range(4):
            for c in range(2):
                last = pe.matmul(pm[q][:, 64 * g:64 * g + 64], probT[q][:, g * 256 + c * P:g * 256 + (c + 1) * P],
                                 vtok[:, bass.ds(blk + c, 1), 64 * kv:64 * kv + 64].rearrange("p a c -> p (a c)"),
                                 start=False, stop=(c == 1), skip_group_check=True)
        last.then_inc(sem("pv_done"), 1)

    def att_out_dve(dve, s):
        q = s.mod(2)
        dve.wait_ge(sem("e_done"), due(s + 1))
        dve.tensor_tensor(stat[:, s.mod(4), 4, :], stat[:, s.mod(4), 2, :], stat[:, s.mod(4), 3, :], ALU.add).then_inc(sem("den"), 1)
        dve.wait_ge(sem("den"), due(s + 1))
        dve.reciprocal(stat[:, s.mod(4), 5, :], stat[:, s.mod(4), 4, :]).then_inc(sem("rden"), 1)
        dve.wait_ge(sem("rden"), due(s + 1))
        dve.wait_ge(sem("pv_done"), due(s + 1))
        dve.wait_ge(sem("ot_done"), due(s + (-1)))
        dve.tensor_tensor(ob[q][:, :].rearrange("p (g d) -> p g d", g=4),
                          pm[q][:, 0:256].rearrange("p (g d) -> p g d", g=4),
                          stat[:, s.mod(4), 5, :].rearrange("p (g a) -> p g a", a=1).to_broadcast([P, 4, HD]), ALU.mult)\
            .then_inc(sem("ob_done"), 1)

    def att_out_turn(pe, s):
        q = s.mod(2)
        pe.wait_ge(sem("ob_done"), due(s + 1))
        for j in range(2):
            last = pe.transpose(pm[q][:, 256 + j * P:256 + (j + 1) * P], ob[q][:, j * P:(j + 1) * P], ident[:, :])
        last.then_inc(sem("ot_done"), 1)

    def att_gate(dve, s):
        kv, q, blk = s.mod(4), s.mod(2), s.div(4)
        c = bass.ds(META + blk * P, P)
        dve.wait_ge(sem("ot_done"), due(s + 1))
        dve.tensor_tensor(og[q][:, :, :], pm[q][:, 256:512].rearrange("p (j c) -> p j c", j=2),
                          gate[:, 2 * kv:2 * kv + 2, c], ALU.mult).then_inc(sem("gated"), 1)

    def att_high(act, s):
        kv, q, blk = s.mod(4), s.mod(2), s.div(4)
        act.wait_ge(sem("gated"), due(s + 1))
        act.activation(oh[:, 2 * kv:2 * kv + 2, bass.ds(META + blk * P, P)], og[q][:, :, :], ACT.Copy)\
            .then_inc(sem("o_hi"), 1)

    def att_low(dve, s):
        kv, q, blk = s.mod(4), s.mod(2), s.div(4)
        c = bass.ds(META + blk * P, P)
        dve.wait_ge(sem("o_hi"), due(s + 1))
        dve.tensor_tensor(ol[:, 2 * kv:2 * kv + 2, c], og[q][:, :, :],
                          oh[:, 2 * kv:2 * kv + 2, c].bitcast(F32), ALU.subtract).then_inc(sem("o_lo"), 1)

    def input_parts(n):
        if n == 0:
            return [(a["meta_tokens"][:, :], 0, META), (a["x_prompt"][0, 0:P - META, :], META, P - META)]
        if n < 8:
            return [(a["x_prompt"][0, n * P - META:(n + 1) * P - META, :], 0, P)]
        return [(a["x_prompt"][0, SEQ - META:SEQ, :], 0, META),
                (a["x_sample"].rearrange("b t d -> (b t) d"), META, NSM)]

    NTT = 9
    rows_of = [P] * 8 + [META + NSM]

    w_in0 = a["swa_w_in"][0].rearrange("(k p) n -> p k n", p=P)
    QOF, KOF, VOF, GOF = 0, D, D + 256, D + 512
    in_cols = [KOF, KOF + P] + [QOF + P * j for j in range(8)] + [VOF, VOF + P]
    in_order = in_cols + [GOF + P * j for j in range(8)]

    HF = [(H % 2, slice(64 * (H % 2), 64 * (H % 2) + 64)) for H in range(NH)]

    def v16(t):
        return t.rearrange("p (h k) -> p h k", h=NH)

    mstat = stat[0:META, :, :, :].rearrange("p a b c -> p (a b c)")

    def meta_pe(pe):
        pe.wait_ge(sem("o_lo"), UNITS)
        for H in range(NH):
            kv, (f, r) = H // 4, HF[H]
            last = pe.matmul(pm[f][0:META, 16 * (H // 2):16 * (H // 2) + 16], kqv[r, 2 + H // 2, 0:META],
                             kb[0][r, kv // 2, 0 if kv % 2 == f else 1, P:P + META], start=True, stop=True)
        last.then_inc(sem("m_scores"), 1)
        pe.wait_ge(sem("m_norm"), 1)
        for H in range(NH):
            last = pe.transpose(ps[0][0:META, 1, 16 * H:16 * H + 16], probM[:, H, :], ident[0:META, 0:META])
        last.then_inc(sem("m_turned"), 1)
        pe.wait_ge(sem("m_tcopied"), 1)
        for H in range(NH):
            kv, r = H // 4, HF[H][1]
            last = pe.matmul(ps[0][r, 0, 16 * (H // 2):16 * (H // 2) + 16], vtok[0:META, 0, 64 * kv:64 * kv + 64],
                             probMT[:, H, :], start=True, stop=True, skip_group_check=True)
        last.then_inc(sem("m_out"), 1)

    def meta_dve(dve):
        dve.wait_ge(sem("m_scores"), 1)
        for f in range(2):
            mm = dve.scalar_tensor_tensor(
                probM[:, :, :].rearrange("p (j f) k -> p j f k", f=2)[:, :, f, :],
                pm[f][0:META, 0:P].rearrange("p (j k) -> p j k", k=META), HD ** -0.5,
                bias[0:META, :, P:P + META].rearrange("p (j f) k -> p j f k", f=2)[:, :, f, :],
                ALU.mult, ALU.add)
        mm.then_inc(sem("m_v"), 1)
        dve.wait_ge(sem("m_v"), 1)
        dve.tensor_reduce(mstat[:, 0:16], probM[:, :, :], AX.X, ALU.max).then_inc(sem("m_v"), 1)
        dve.wait_ge(sem("m_v"), 2)
        dve.tensor_tensor(mstat[:, 0:16], mstat[:, 0:16], sinkb[0:META, :], ALU.max).then_inc(sem("m_v"), 1)
        dve.wait_ge(sem("m_v"), 3)
        dve.tensor_tensor(mstat[:, 16:32], sinkb[0:META, :], mstat[:, 0:16], ALU.subtract).then_inc(sem("m_v"), 1)
        dve.tensor_tensor(probM[:, :, :], probM[:, :, :],
                          mstat[:, 0:16].rearrange("p (h a) -> p h a", a=1).to_broadcast([META, NH, META]),
                          ALU.subtract).then_inc(sem("m_v"), 1)
        dve.wait_ge(sem("m_exp"), 1)
        dve.tensor_reduce(mstat[:, 32:48], probM[:, :, :], AX.X, ALU.add).then_inc(sem("m_v"), 1)
        dve.wait_ge(sem("m_v"), 6)
        dve.tensor_tensor(mstat[:, 32:48], mstat[:, 32:48], mstat[:, 16:32], ALU.add).then_inc(sem("m_v"), 1)
        dve.wait_ge(sem("m_v"), 7)
        dve.reciprocal(mstat[:, 32:48], mstat[:, 32:48]).then_inc(sem("m_v"), 1)
        dve.wait_ge(sem("m_v"), 8)
        dve.tensor_tensor(probM[:, :, :], probM[:, :, :],
                          mstat[:, 32:48].rearrange("p (h a) -> p h a", a=1).to_broadcast([META, NH, META]),
                          ALU.mult).then_inc(sem("m_norm"), 1)
        dve.wait_ge(sem("m_turned"), 1)
        dve.tensor_copy(probMT[:, :, :], v16(ps[0][0:META, 1, 0:256])).then_inc(sem("m_tcopied"), 1)
        dve.wait_ge(sem("m_out"), 1)
        dve.tensor_tensor(og[0][:, :, :].rearrange("p a c -> p (a c)")[:, 0:P].rearrange("p (j c) -> p j c", c=META),
                          ps[0][:, 0, 0:P].rearrange("p (j c) -> p j c", c=META), gate[:, :, 0:META], ALU.mult)\
            .then_inc(sem("m_gated"), 1)
        dve.wait_ge(sem("m_hi"), 1)
        dve.tensor_tensor(ol[:, :, 0:META], og[0][:, :, :].rearrange("p a c -> p (a c)")[:, 0:P]
                          .rearrange("p (j c) -> p j c", c=META), oh[:, :, 0:META].bitcast(F32), ALU.subtract)\
            .then_inc(sem("m_lo"), 1)

    def meta_act(act):
        act.wait_ge(sem("m_v"), 5)
        act.activation(mstat[:, 16:32], mstat[:, 16:32], ACT.Exp)
        act.activation(probM[:, :, :], probM[:, :, :], ACT.Exp).then_inc(sem("m_exp"), 1)
        act.wait_ge(sem("m_gated"), 1)
        act.activation(oh[:, :, 0:META], og[0][:, :, :].rearrange("p a c -> p (a c)")[:, 0:P]
                       .rearrange("p (j c) -> p j c", c=META), ACT.Copy).then_inc(sem("m_hi"), 1)

    def samp_loads(sp, b):
        q = b.mod(2)
        sp.wait_ge(sem("sa_out"), due(b + (-1)))
        one = bass.ds(b.v, 1)
        for dst, src in ((kc[q], a["cache_swa_k"][0, one]), (vc[q], a["cache_swa_v"][0, one]),
                         (kmt[q], a["cache_swa_meta_k"][0, one]), (vmt[q], a["cache_swa_meta_v"][0, one])):
            sp.dma_start(dst[:, :], src.rearrange("a t h d -> (a t) (h d)")).then_inc(sem(f"sa_in{q}"), 16)
        sp.dma_start(vnt[q][:, :], vnew_d[one].rearrange("a t c -> (a t) c")).then_inc(sem(f"sa_in{q}"), 16)

    def samp_queries_dve(dve, b):
        q = b.mod(2)
        dve.wait_ge(sem("sa_scores"), due(b + (-1)))
        c = bass.ds(NPR + b.v * DECT, DECT)
        for f in range(2):
            r = slice(64 * f, 64 * f + 64)
            for kv in range(KVH):
                dst = qsb[q][:, kv, 0:16].rearrange("d (a f t) -> d a f t", f=2, t=DECT)[:, :, f, :]
                dve.tensor_copy(dst, kqv[r, 2 + 2 * kv:4 + 2 * kv, c])
            last = dve.tensor_copy(ktb[q][:, :, META + WIN:SKEYS].rearrange("d (a f) t -> d a f t", f=2)[:, :, f, :],
                                   kqv[r, 0:2, c])
        last.then_inc(sem("sa_q"), 1)

    def samp_turn_keys(pe, b):
        q = b.mod(2)
        wait_apart(pe, sem(f"sa_in{q}"), 80 * b.div(2) + 80)
        wait_apart(pe, sem("sa_keys"), b)
        for kv in range(KVH):
            pe.transpose(ps[0][0:64, 0, kv * P:(kv + 1) * P], kc[q][:, 64 * kv:64 * kv + 64], ident[:, :])
        for kv in range(KVH):
            last = pe.transpose(ps[0][0:64, 1, kv * META:(kv + 1) * META], kmt[q][:, 64 * kv:64 * kv + 64],
                                ident[0:META, 0:META])
        last.then_inc(sem("sa_kt"), 1)

    def samp_keys_act(act, b):
        q = b.mod(2)
        act.wait_ge(sem("sa_kt"), due(b + 1))
        act.wait_ge(sem("sa_scores"), due(b + (-1)))
        act.activation(ktb[q][:, :, META:META + WIN], ps[0][0:64, 0, :].rearrange("d (h k) -> d h k", h=KVH), ACT.Copy)
        act.activation(ktb[q][:, :, 0:META], ps[0][0:64, 1, 0:64].rearrange("d (h k) -> d h k", h=KVH), ACT.Copy)\
            .then_inc(sem("sa_keys"), 1)

    def samp_scores(pe, b):
        q = b.mod(2)
        wait_apart(pe, sem("sa_keys"), b + 1)
        pe.wait_ge(sem("sa_q"), due(b + 1))
        pe.wait_ge(sem("sa_biased"), due(b))
        for kv in range(KVH):
            last = pe.matmul(ps[1][32 * kv:32 * kv + 32, 0, 0:SKEYS], qsb[q][:, kv, :], ktb[q][:, kv, :],
                             start=True, stop=True)
        last.then_inc(sem("sa_scores"), 1)

    def samp_softmax_dve(dve, b):
        q = b.mod(2)
        st = sstat[:, q, :]
        dve.wait_ge(sem("sa_scores"), due(b + 1))
        dve.wait_ge(sem("sa_pt"), due(b + (-1)))
        dve.scalar_tensor_tensor(probS[q][:, :], ps[1][:, 0, 0:SKEYS], HD ** -0.5, biasS[:, :], ALU.mult, ALU.add)\
            .then_inc(sem("sa_biased"), 1)
        dve.wait_ge(sem("sa_biased"), due(b + 1))
        dve.tensor_reduce(st[:, 0:1], probS[q][:, :], AX.X, ALU.max).then_inc(sem("sa_max"), 1)
        dve.wait_ge(sem("sa_max"), due(b + 1))
        dve.scalar_tensor_tensor(st[:, 1:2], st[:, 0:1], -1.0, sinks[:, 1:2], ALU.mult, ALU.min).then_inc(sem("sa_nmax"), 1)

    def samp_exp(act, b):
        q = b.mod(2)
        st = sstat[:, q, :]
        act.wait_ge(sem("sa_nmax"), due(b + 1))
        act.activation(probS[q][:, :], probS[q][:, :], ACT.Exp, bias=st[:, 1:2], accum_out=st[:, 2:3])
        act.activation(st[:, 3:4], sinks[:, 0:1], ACT.Exp, bias=st[:, 1:2]).then_inc(sem("sa_exp"), 1)

    SSEG = ((0, 0, META), (1, META, WIN), (2, META + WIN, DECT))

    def samp_turn(pe, b):
        q = b.mod(2)
        pe.wait_ge(sem("sa_exp"), due(b + 1))
        wait_apart(pe, sem("sa_ptc"), b)
        for j, k0, n in SSEG:
            last = pe.transpose(ps[1][0:n, 1, j * P:(j + 1) * P], probS[q][:, k0:k0 + n], ident[:, :])
        last.then_inc(sem("sa_pt"), 1)

    def samp_turned_act(act, b):
        q = b.mod(2)
        act.wait_ge(sem("sa_pt"), due(b + 1))
        act.wait_ge(sem("sa_pv"), due(b + (-1)))
        for j, k0, n in SSEG:
            last = act.activation(pts[q][0:n, j, :], ps[1][0:n, 1, j * P:(j + 1) * P], ACT.Copy)
        last.then_inc(sem("sa_ptc"), 1)

    def samp_values(pe, b):
        q = b.mod(2)
        wait_apart(pe, sem("sa_ptc"), b + 1)
        wait_apart(pe, sem("sa_gated"), b + (-1))
        for kv in range(KVH):
            for j, k0, n in SSEG:
                v = (vmt, vc, vnt)[j][q]
                last = pe.matmul(pm[q][32 * kv:32 * kv + 32, 0:HD], pts[q][0:n, j, 32 * kv:32 * kv + 32],
                                 v[0:n, 64 * kv:64 * kv + 64], start=(j == 0), stop=(j == 2))
        last.then_inc(sem("sa_pv"), 1)

    def samp_out_dve(dve, b):
        q = b.mod(2)
        st = sstat[:, q, :]
        dve.wait_ge(sem("sa_exp"), due(b + 1))
        dve.tensor_tensor(st[:, 4:5], st[:, 2:3], st[:, 3:4], ALU.add).then_inc(sem("sa_den"), 1)
        dve.wait_ge(sem("sa_den"), due(b + 1))
        dve.reciprocal(st[:, 5:6], st[:, 4:5]).then_inc(sem("sa_rden"), 1)
        dve.wait_ge(sem("sa_rden"), due(b + 1))
        dve.wait_ge(sem("sa_pv"), due(b + 1))
        dve.wait_ge(sem("sa_ot"), due(b + (-1)))
        dve.tensor_scalar(obS[q][:, :], pm[q][:, 0:HD], st[:, 5:6], None, ALU.mult).then_inc(sem("sa_out"), 1)

    def samp_out_turn(pe, b):
        q = b.mod(2)
        wait_apart(pe, sem("sa_out"), b + 1)
        pe.transpose(pm[q][0:HD, P:2 * P], obS[q][:, :], ident[:, :]).then_inc(sem("sa_ot"), 1)

    def samp_gate(dve, b):
        q = b.mod(2)
        dve.wait_ge(sem("sa_ot"), due(b + 1))
        for f in range(2):
            r = slice(64 * f, 64 * f + 64)
            for kv in range(KVH):
                src = pm[q][0:HD, P + 32 * kv:P + 32 * kv + 16].rearrange("d (a f t) -> d a f t", f=2, t=DECT)[:, :, f, :]
                last = dve.tensor_tensor(ogS[r, 2 * kv:2 * kv + 2, bass.ds(b.v * DECT, DECT)], src,
                                         gate[r, 2 * kv:2 * kv + 2, bass.ds(NPR + b.v * DECT, DECT)], ALU.mult)
        last.then_inc(sem("sa_gated"), 1)

    NS0, NS1 = 20, 8

    TURNS = [(10, 0, META)] + [(10, META + P * i, P) for i in range(NBLK)] + [(10, NPR, NSM)] \
        + [(0, 0, META), (0, META + P * (NBLK - 1), P), (0, NPR, NSM)]

    def turn_pe(pe):
        for n, (t, c, r) in enumerate(TURNS):
            pe.wait_ge(sem("tk_copied"), due(n - 1))
            for j in range(2):
                last = pe.transpose(ps[n % 2][0:r, 0, j * P:(j + 1) * P], kqv[:, t + j, c:c + r], ident[:, :])
            last.then_inc(sem("tk_turned"), 1)

    def turn_dve(dve):
        for n, (t, c, r) in enumerate(TURNS):
            dve.wait_ge(sem("tk_turned"), due(n + 1))
            dst = vtok[0:r, n, :] if t == 10 else ktok[0:r, n - 10, :]
            dve.tensor_copy(dst, ps[n % 2][0:r, 0, 0:256]).then_inc(sem("tk_copied"), 1)

    L1S, L1T = NS0 + NS1, NS0 + NS1
    HS, HT = 18, 24
    w_in1 = a["mlstm_w_in"][0].rearrange("(k p) n -> p k n", p=P)

    def heads(eng, body):
        body(eng, 0)
        with eng.Fori(1, MH - 1) as h:
            body(eng, h)
        body(eng, MH - 1)

    def p1_source(h, j):
        if j < 12:
            off = (INNER, 2 * INNER, 0)[j % 3] + P * (j // 3)
            return w_in1[:, :, bass.ds(off + MD * h, P)], KT
        w = a[("mlstm_wv", "mlstm_wq", "mlstm_wk")[(j - 12) // 2]][0]
        c = 256 * (j % 2)
        src = w[bass.ds(h, 1)].rearrange("a (k p) n -> p (a k) n", p=P)
        return src[:, :, c:c + 256], 4

    def slot1(h, j):
        return Idx(L1S + j, h, HS)

    def tile1(h, i):
        return Idx(L1T + i, h, HT)

    def tile_of(j):
        return j if j < 12 else 12 + 2 * (j - 12)

    def p1_sp(sp, h):
        for j in range(HS):
            if isinstance(h, int) and h == 0 and j < 3:
                continue
            src, k = p1_source(h, j)
            slot_load(sp, slot1(h, j), src, k)
            if j == 6:
                sp.wait_ge(sem("gate_mm"), 12 * h)
                sp.wait_ge(sem("gate_zero"), 1)
                for i, part in enumerate((2, 0, 1)):
                    for f in range(2):
                        rows = a["mlstm_w_gates"][0, bass.ds(part * INNER + MD * h, MD), 4 * f:4 * f + 4]
                        sp.dma_start(wg[:, 4 * i:4 * i + 4, 32 * f:32 * f + 4],
                                     rows.rearrange("(k p) c -> p k c", p=P)).then_inc(sem("wg_in"), 16)

    def p1_store(eng, h, t, which):
        if which == 0:
            eng.wait_ge(sem("ga_done"), 4 * h + t + 1)
            eng.dma_start(ga_d[bass.ds(4 * h + t, 1)].rearrange("a p c -> p (a c)"), st[1][:, 0, :]).then_inc(sem("st1_out"), 16)
        else:
            eng.wait_ge(sem("gb_done"), 4 * h + t + 1)
            eng.dma_start(gb_d[bass.ds(4 * h + t, 1)].rearrange("a p c -> p (a c)"), st[2][:, 0, :]).then_inc(sem("st2_out"), 16)

    def p1_gp(gp, h):
        for t in range(4):
            gp.wait_ge(sem("ctx_free"), due(4 * h + t - 1))
            gp.tensor_copy(smp(xr[t % 2])[:, :, 0:CW - 1],
                           cstate[:, bass.ds(4 * h + t, 1), :].rearrange("p a (b w) -> p (a b) w", b=DECB))\
                .then_inc(sem("ctx"), 1)
            gp.wait_ge(sem("xm_in"), 4 * h + t + 1)
            gp.wait_ge(sem("ctx"), 4 * h + t + 1)
            dst = ctail[:, bass.ds(4 * h + t, 1), :].rearrange("p a c -> p (a c)")
            gp.tensor_copy(dst[:, 0:CW - 1], xr[t % 2][:, NPR:XPR])
            gp.tensor_copy(dst[:, CW - 1:27].rearrange("p (b w) -> p b w", b=DECB),
                           smp(xr[t % 2])[:, :, DECT:DECT + CW - 1]).then_inc(sem("tail_saved"), 1)

    def smp(x):
        return x[:, XPR:XPR + DECB * (CW - 1 + DECT)].rearrange("p (b t) -> p b t", b=DECB)

    def p1_pe(pe, h):
        for j in range(HS):
            n = slot1(h, j)
            if j < 12:
                product(pe, n, tile1(h, j), KT, 0, h1h, h1l, made=KT if isinstance(h, int) and h == 0 and j == 0 else None)
                continue
            ah, al = (xmh, xml) if j < 14 else (xch, xcl)
            if j == 14:
                pe.wait_ge(sem("xc_lo"), 4 * h + 4)
            if j == 12:
                pe.wait_ge(sem("xm_lo"), 4 * h + 4)
                pe.wait_ge(sem("wg_in"), 96 * h + 96)
            for c in range(2):
                i = 2 * (j - 12) + c
                product(pe, n, tile1(h, 12 + i), 4, c, ah, al)
                if i > 0:
                    gate_mm(pe, h, i - 1)
        gate_mm(pe, h, 11)

    def gate_mm(pe, h, i):
        pe.wait_ge(sem("qkv_ev"), 12 * h + i + 1)
        for g in range(3):
            r = 64 if g == 1 else 0
            last = pe.matmul(pm[g // 2][r:r + 36, 0:GRP], wg[:, i, :], st[i % 3][:, 0, g * GRP:(g + 1) * GRP],
                             start=False, stop=False, skip_group_check=True)
        last.then_inc(sem("gate_mm"), 1)

    def p1_act(act, h):
        def convolved(t):
            act.wait_ge(sem("conv_done"), 4 * h + t + 1)
            act.activation(xc[t % 2][:, 0, :], xc[t % 2][:, 0, :], ACT.Silu).then_inc(sem("xc_done"), 1)
            act.wait_ge(sem("xc_done"), 4 * h + t + 1)
            act.activation(xch[:, t, :], xc[t % 2][:, 0, :], ACT.Copy).then_inc(sem("xc_hi"), 1)

        for j in range(HS):
            t, s = j // 3, j % 2
            if j < 12:
                full = ps[s][:, :, 0:GRP]
                act.wait_ge(sem("ps_full"), due(tile1(h, j) + 1))
                if j % 3 == 0:
                    if t > 0:
                        p1_store(act, h, t - 1, 1)
                    act.wait_ge(sem("gb_done"), due(4 * h + t - 1))
                    act.activation(v3(sz[t % 2][:, 0, :]), full, ACT.Silu).then_inc(sem("sz_done"), 1)
                    act.wait_ge(sem("sz_done"), 4 * h + t + 1)
                    act.sem_inc(sem(f"ps_free{s}"), 1)
                elif j % 3 == 1:
                    act.wait_ge(sem("ga_done"), 4 * h + t)
                    if t == 0:
                        act.wait_ge(sem("st0_out"), 64 * h)
                        act.wait_ge(sem("gate_mm"), 12 * h)
                    act.activation(v3(st[0][:, 0, :]), full, ACT.Sigmoid).then_inc(sem("sg_done"), 1)
                    act.wait_ge(sem("sg_done"), 4 * h + t + 1)
                    act.sem_inc(sem(f"ps_free{s}"), 1)
                else:
                    p1_store(act, h, t, 0)
                    if t == 0:
                        act.wait_ge(sem("ps_full"), due(tile1(h, 0)))
                    act.activation(v3(xmh[:, t, :]), full, ACT.Copy).then_inc(sem("xm_hi"), 1)
                    act.wait_ge(sem("conv_done"), due(4 * h + t - 1))
                    act.wait_ge(sem("tail_saved"), due(4 * h + t - 1))
                    x = xr[t % 2]
                    act.activation(x[:, CW - 1:CW - 1 + 2 * GRP].rearrange("p (g c) -> p g c", g=2), ps[s][:, 0:2, 0:GRP], ACT.Copy)
                    act.activation(x[:, CW - 1 + 2 * GRP:XPR], ps[s][:, 2, 0:NPR - 2 * GRP], ACT.Copy)
                    act.activation(smp(x)[:, :, CW - 1:],
                                   ps[s][:, 2, NPR - 2 * GRP:T - 2 * GRP].rearrange("p (b t) -> p b t", b=DECB), ACT.Copy)\
                        .then_inc(sem("xm_in"), 1)
                split_hi(act, slot1(h, j + 3), tile1(h, tile_of(j)) + 1)
                if j % 3 == 2 and t < 3:
                    convolved(t)
                continue
            for c in range(2):
                i = 2 * (j - 12) + c
                m, b = tile1(h, 12 + i), i % 3
                act.wait_ge(sem("ps_full"), due(m + 1))
                if i < 3:
                    if i == 0:
                        act.wait_ge(sem("ga_done"), 4 * h + 4)
                    else:
                        act.wait_ge(sem(f"st{b}_out"), 128 * h + 64)
                else:
                    act.wait_ge(sem("gate_mm"), due(12 * h + i - 2))
                    act.wait_ge(sem(f"st{b}_out"), due((64 if b == 0 else 128) * h + (0 if b == 0 else 64) + 16 * (i // 3)))
                act.activation(v3(st[b][:, 0, :]), ps[c][:, :, 0:GRP], ACT.Copy,
                               scale=(MD ** -0.5 if i // 4 == 2 else 1.0)).then_inc(sem("qkv_ev"), 1)
                act.wait_ge(sem("qkv_ev"), 12 * h + i + 1)
                act.sem_inc(sem(f"ps_free{c}"), 1)
                act.dma_start((v_d, q_d, k_d)[i // 4][bass.ds(4 * h + i % 4, 1)].rearrange("a p c -> p (a c)"),
                              st[b][:, 0, :]).then_inc(sem(f"st{b}_out"), 16)
            if j == 12:
                convolved(3)
                p1_store(act, h, 3, 1)
            if not (j + 3 >= HS and isinstance(h, int) and h == MH - 1):
                split_hi(act, slot1(h, j + 3), tile1(h, tile_of(j) + 1) + 1)

    def p1_dve(dve, h):
        dve.tensor_copy(hvec[:, :, :], vcol[:, 16:P].rearrange("p (w k) -> p w k", k=16)[:, :, bass.ds(4 * h, 4)])\
            .then_inc(sem("hvec"), 1)
        dve.wait_ge(sem("hvec"), h + 1)
        for j in range(HS):
            if j >= 12 or j % 3 != 2:
                if not (j + 3 >= HS and isinstance(h, int) and h == MH - 1):
                    split_lo(dve, slot1(h, j + 3))
            t = j // 3
            if j >= 12:
                continue
            c = 4 * h + t
            K4 = 4 * h + t + 1
            if j % 3 == 1:
                dve.wait_ge(sem("sg_done"), K4)
                dve.wait_ge(sem("sz_done"), K4)
                dve.wait_ge(sem("st1_out"), 128 * h + 16 * t)
                if t == 0:
                    dve.wait_ge(sem("gate_mm"), 12 * h)
                dve.scalar_tensor_tensor(st[1][:, 0, :], st[0][:, 0, :], hnorm_h[:, t:t + 1], sz[t % 2][:, 0, :],
                                         ALU.mult, ALU.mult).then_inc(sem("ga_done"), 1)
            if j % 3 == 2:
                s = j % 2
                dve.wait_ge(sem("xm_hi"), K4)
                dve.wait_ge(sem("xm_in"), K4)
                dve.wait_ge(sem("ctx"), K4)
                dve.tensor_tensor(v3(xml[:, t, :]), ps[s][:, :, 0:GRP], v3(xmh[:, t, :].bitcast(F32)), ALU.subtract)\
                    .then_inc(sem("xm_lo"), 1)
                dve.wait_ge(sem("xm_lo"), K4)
                dve.sem_inc(sem(f"ps_free{s}"), 1)
                split_lo(dve, slot1(h, j + 3))
                x, y = xr[t % 2], xc[t % 2]
                dve.wait_ge(sem("xc_lo"), due(4 * h + t - 1))
                xs, ys = smp(x), y[:, 0, NPR:T].rearrange("p (b t) -> p b t", b=DECB)
                for w in range(CW):
                    cw = convw_h[:, w, t:t + 1]
                    if w == 0:
                        dve.tensor_scalar(y[:, 0, 0:NPR], x[:, w:w + NPR], cw, convb_h[:, t:t + 1], ALU.mult, ALU.add)
                        last = dve.tensor_scalar(ys, xs[:, :, w:w + DECT], cw, convb_h[:, t:t + 1], ALU.mult, ALU.add)
                    else:
                        dve.wait_ge(sem("conv_step"), due(4 * c + w if isinstance(c, int) else 16 * h + 4 * t + w))
                        dve.scalar_tensor_tensor(y[:, 0, 0:NPR], x[:, w:w + NPR], cw, y[:, 0, 0:NPR], ALU.mult, ALU.add)
                        last = dve.scalar_tensor_tensor(ys, xs[:, :, w:w + DECT], cw, ys, ALU.mult, ALU.add)
                    last.then_inc(sem("conv_step"), 1)
                dve.wait_ge(sem("conv_step"), 16 * h + 4 * t + 4)
                dve.sem_inc(sem("conv_done"), 1)
                dve.sem_inc(sem("ctx_free"), 1)
                dve.wait_ge(sem("xc_done"), K4)
                dve.wait_ge(sem("st2_out"), 128 * h + 16 * t)
                if t == 0:
                    dve.wait_ge(sem("gate_mm"), 12 * h)
                dve.scalar_tensor_tensor(st[2][:, 0, :], y[:, 0, :], skip_h[:, t:t + 1], sz[t % 2][:, 0, :],
                                         ALU.mult, ALU.mult).then_inc(sem("gb_done"), 1)
                dve.wait_ge(sem("xc_hi"), K4)
                dve.tensor_tensor(xcl[:, t, :], y[:, 0, :], xch[:, t, :].bitcast(F32), ALU.subtract).then_inc(sem("xc_lo"), 1)

    S1 = 1 + NPR
    BS = DECT + 1

    def sfirst(x, at=0):
        return x[:, S1 + at:S1 + at + BS * (DECB - 1) + 1:BS]

    def stok(x):
        return x[:, S1:ICOL].rearrange("r (b t) -> r b t", b=DECB)[:, :, 1:BS]

    def blocks(x):
        return x[:, 1 + META:1 + NPR].rearrange("r (b t) -> r b t", b=NBLK)

    def bc(x, shape):
        return x.rearrange("r (b a) -> r b a", a=1).to_broadcast(shape)

    def gates_sp(sp):
        for r in (0, 64):
            for f in range(2):
                sp.dma_start(brow[r + 32 * f:r + 32 * f + MH, :], dram(a["mlstm_b_gates"], MH * f, [[1, MH], [1, 1]]))\
                    .then_inc(sem("cell_in"), 16)
        sp.dma_start(tri[:, :], a["c_tri"]).then_inc(sem("cell_in"), 16)
        sp.dma_start(trism[:, :], a["c_trism"]).then_inc(sem("cell_in"), 16)
        sp.dma_start(blkm[:, :], a["c_blkm"]).then_inc(sem("cell_in"), 16)
        sp.dma_start(snin[:, :], a["state_mlstm_n"][0].rearrange("b h d -> (b h) d")).then_inc(sem("cell_in"), 16)
        sp.wait_ge(sem("row_zero"), 5)
        sp.dma_start(sfirst(gi), dram(a["state_mlstm_m"], 0, [[1, MH], [MH, DECB], [1, 1]]),
                     allow_slow_non_contiguous=True).then_inc(sem("m0_in"), 16)
        sp.dma_start(o["prompt_conv"][0, 0], orow[0:3, :]).then_inc(sem("orow_out"), 16)
        sp.dma_start(o["sample_conv"][0].rearrange("b w c -> (b w) c"), orow[3:27, :]).then_inc(sem("orow_out"), 16)
        for c in (NCH - 1, 0, 1, 2):
            chunk_load(sp, 0, c)
        sp.wait_ge(sem("a_row"), 1)
        sp.dma_start(arow_d, fx[:, :]).then_inc(sem("rows_out"), 16)
        sp.wait_ge(sem("decay"), 1)
        sp.dma_start(srow_d[0], scal[:, 0, :]).then_inc(sem("rows_out"), 16)
        sp.dma_start(srow_d[1], scal[:, 4, :]).then_inc(sem("rows_out"), 16)
        sp.wait_ge(sem("w_samp"), 1)
        sp.dma_start(wrow_d, wrow[:, :]).then_inc(sem("rows_out"), 16)
        sp.dma_start(o["prompt_mlstm_m"][0, 0].rearrange("(h a) -> h a", a=1), mm_[:, NPR:NPR + 1]).then_inc(sem("m_out"), 16)
        sp.dma_start(dram(o["sample_mlstm_m"], 0, [[1, MH], [MH, DECB], [1, 1]]),
                     scal[:, 1, NBLK + 1:].rearrange("h (b a) -> h b a", a=1),
                     allow_slow_non_contiguous=True).then_inc(sem("m_out"), 16)
        sp.wait_ge(sem("rows_out"), 64)
        sp.dma_start(bcs[:, :, :, :], dram(srow_d, 0, [[0, P], [MH * 17, 2], [17, MH], [1, 17]])).then_inc(sem("rows_in"), 16)
        sp.dma_start(wsb[:, :, :], dram(wrow_d, 0, [[0, P], [NSM, MH], [1, NSM]])).then_inc(sem("rows_in"), 16)
        for h in range(MH):
            sp.dma_start(absm[:, h, :].rearrange("p (b t) -> p b t", b=DECB),
                         dram(arow_d, h * ICOL + S1 + 1, [[0, NSM], [BS, DECB], [1, DECT]])).then_inc(sem("rows_in"), 16)
        sp.wait_ge(sem("m_out"), 32)
        sp.wait_ge(sem("col_done"), 1)

    def gates_gp(gp):
        steps = [(gi[:, :], 0.0), (fx[:, :], 0.0), (msk[:, :], 1.0), (msk[:, 0:2], 0.0), (blocks(msk)[:, :, 0], 0.0),
                 (sfirst(msk), 0.0), (sfirst(msk, 1), 0.0), (rs[:, :], 0.0), (col[:, :, :], 0.0)]
        for n, (t, v) in enumerate(steps):
            gp.wait_ge(sem("row_zero"), due(n))
            gp.memset(t, v).then_inc(sem("row_zero"), 1)
        gp.wait_ge(sem("row_zero"), due(len(steps)))
        gp.wait_ge(sem("orow_out"), 32)
        for n, t in enumerate((uh, ul)):
            gp.wait_ge(sem("u_zero"), due(n))
            gp.memset(t[:, :, T:TP].bitcast(F32), 0.0).then_inc(sem("u_zero"), 1)
        gp.wait_ge(sem("u_zero"), 2)

    def gates_dve(dve):
        dve.wait_ge(sem("row_zero"), 9)
        dve.wait_ge(sem("m0_in"), 16)
        dve.wait_ge(sem("cell_in"), 16 * 8)
        step = [0]

        def done(ins):
            ins.then_inc(sem("row_step"), 1)
            step[0] += 1
            dve.wait_ge(sem("row_step"), step[0])

        for f, dst in ((0, gi), (1, fx)):
            for g in range(2):
                r = 64 * g + 32 * f
                done(dve.tensor_scalar(dst[:, 1 + g * GRP:1 + (g + 1) * GRP], pm[0][r:r + MH, 0:GRP], brow[r:r + MH, 0:1],
                                       None, ALU.add))
            r = 32 * f
            n = NPR - 2 * GRP
            done(dve.tensor_scalar(dst[:, 1 + 2 * GRP:1 + NPR], pm[1][r:r + MH, 0:n], brow[r:r + MH, 0:1], None, ALU.add))
            done(dve.tensor_scalar(stok(dst), pm[1][r:r + MH, n:n + NSM].rearrange("r (b t) -> r b t", b=DECB),
                                   brow[r:r + MH, 0:1], None, ALU.add))
        dve.scalar_tensor_tensor(cb[:, :], fx[:, :], -1.0, fx[:, :], ALU.mult, ALU.max).then_inc(sem("f_abs"), 1)
        dve.wait_ge(sem("f_ln"), 1)
        done(dve.scalar_tensor_tensor(lf[:, :], fx[:, :], 0.0, cb[:, :], ALU.min, ALU.subtract))
        done(dve.tensor_tensor_scan(cb[:, :], msk[:, :], lf[:, :], 0.0, ALU.mult, ALU.add))
        done(dve.memset(lf[:, 0:1], NEG))
        done(dve.memset(sfirst(lf), NEG))
        done(dve.tensor_tensor_scan(mm_[:, :], lf[:, :], gi[:, :], 0.0, ALU.add, ALU.max))
        dve.tensor_tensor(fx[:, :], cb[:, :], mm_[:, :], ALU.subtract).then_inc(sem("a_row"), 1)
        done(dve.tensor_tensor(rs[0:MH, :], gi[:, :], cb[:, :], ALU.subtract))
        last = slice(META, META + P * NBLK + 1, P)
        done(dve.tensor_copy(scal[:, 0, 0:1], mm_[:, 0:1]))
        done(dve.tensor_copy(scal[:, 0, 1:NBLK + 1], mm_[:, META:META + P * (NBLK - 1) + 1:P]))
        done(dve.tensor_copy(scal[:, 0, NBLK + 1:], sfirst(mm_)))
        done(dve.tensor_copy(scal[:, 1, 0:NBLK + 1], mm_[:, last]))
        done(dve.tensor_copy(scal[:, 1, NBLK + 1:], sfirst(mm_, DECT)))
        done(dve.tensor_copy(scal[:, 2, 0:NBLK + 1], cb[:, last]))
        done(dve.tensor_copy(scal[:, 2, NBLK + 1:], sfirst(cb, DECT)))
        done(dve.tensor_tensor(scal[:, 3, :], scal[:, 2, :], scal[:, 1, :], ALU.subtract))
        dve.tensor_tensor(scal[:, 4, :], scal[:, 3, :], scal[:, 0, :], ALU.add).then_inc(sem("decay_arg"), 1)
        done(dve.tensor_scalar(gi[:, 0:1 + META], rs[0:MH, 0:1 + META], scal[:, 3, 0:1], None, ALU.add))
        done(dve.tensor_tensor(blocks(gi), blocks(rs[0:MH]), bc(scal[:, 3, 1:NBLK + 1], [MH, NBLK, P]), ALU.add))
        done(dve.tensor_tensor(stok(gi), stok(rs[0:MH]), bc(scal[:, 3, NBLK + 1:], [MH, DECB, DECT]), ALU.add))
        dve.wait_ge(sem("a_row"), 1)
        done(dve.tensor_tensor(wrow[:, :].rearrange("r (b t) -> r b t", b=DECB), stok(fx),
                               bc(scal[:, 0, NBLK + 1:], [MH, DECB, DECT]), ALU.add))
        dve.sem_inc(sem("exp_args"), 1)
        dve.wait_ge(sem("rs_done"), 2)
        dve.tensor_copy(rss[:, :].rearrange("r (b t) -> r b t", b=DECB), stok(rs)).then_inc(sem("rss"), 1)
        dve.wait_ge(sem("col_t"), 1)
        done(dve.tensor_copy(col[0:META, 0, :], ps[0][0:META, 0, 0:P]))
        done(dve.tensor_copy(col[:, 1:4, :].rearrange("p c x -> p (c x)"), ps[0][:, 0, P:4 * P]))
        done(dve.tensor_copy(col[:, 4:8, :].rearrange("p c x -> p (c x)"), ps[0][:, 1, :]))
        done(dve.tensor_copy(col[:, 8, :], ps[0][:, 2, 0:P]))
        done(dve.tensor_copy(col[0:NSM, 9, :], ps[0][0:NSM, 2, P:2 * P]))
        done(dve.tensor_copy(sn[:, :, :].rearrange("p k c -> p (k c)"), ps[1][:, 0, 0:P]))
        dve.sem_inc(sem("col_done"), 1)

    def gates_act(act):
        act.wait_ge(sem("f_abs"), 1)
        act.activation(cb[:, :], cb[:, :], ACT.Exp, scale=-1.0).then_inc(sem("f_exp"), 1)
        act.wait_ge(sem("f_exp"), 1)
        act.activation(cb[:, :], cb[:, :], ACT.Ln, bias=ones[0:MH, 0:1]).then_inc(sem("f_ln"), 1)
        act.wait_ge(sem("decay_arg"), 1)
        act.activation(scal[:, 4, :], scal[:, 4, :], ACT.Exp).then_inc(sem("decay"), 1)
        act.wait_ge(sem("exp_args"), 1)
        act.activation(wrow[:, :], wrow[:, :], ACT.Exp).then_inc(sem("w_samp"), 1)
        act.activation(rs[32:32 + MH, :], gi[:, :], ACT.Exp).then_inc(sem("rs_done"), 1)
        act.activation(rs[64:64 + MH, :], mm_[:, :], ACT.Exp, scale=-1.0).then_inc(sem("rs_done"), 1)

    def gates_pe(pe):
        pe.wait_ge(sem("cell_in"), 16 * 8)
        for k in range(4):
            pe.transpose(ps[1][:, 0, 32 * k:32 * k + 32], snin[:, k * P:(k + 1) * P], ident[0:32, 0:32])
        pe.wait_ge(sem("rss"), 1)
        for c in range(NCH):
            src = rs[:, 1:1 + META] if c == 0 else rss[:, :] if c == NCH - 1 else rs[:, 1 + META + P * (c - 1):1 + META + P * c]
            n = src.shape[1]
            last = pe.transpose(ps[0][0:n, c // 4, (c % 4) * P:(c % 4) * P + P], src, ident[:, :])
        last.then_inc(sem("col_t"), 1)

    NP = NBLK + 1
    ROWN = [META] + [P] * NBLK + [NSM]
    COL0 = [0] + [META + P * i for i in range(NBLK)] + [NPR]
    S_, KT_, VT_ = ps[0][:, 0, :], ps[0][:, 1, :], ps[0][:, 2, :]
    U_ = [ps[1][:, 0, :], ps[1][:, 1, :]]
    SM = ps[1][:, 2, :]
    NZ = NP + 1
    NU = 4 * NP + 5 * DECB

    CELL_STEPS = 5 * NCH + NP + 4

    def u_tile(c, sample, k):
        return (k if c == 0 else 9 * c - 5 + k) + (5 if sample else 0)

    def num_tile(b):
        return u_tile(b + 1, True, 0) - 1

    def pre_no(c):
        return 0 if c == NCH - 1 else c + 1

    def used(h, c):
        return NU * h + (u_tile(c - 2, False, 3) + 1 if c > 1 else 0)

    def samp_used(h, b):
        return NU * h + (u_tile(b - 1, True, 3) + 1 if b > 1 else 0)

    def chunk_in(c):
        return smin if c == NCH - 1 else chin[c % 3]

    def wait_chunk(eng, h, c):
        if c == NCH - 1:
            eng.wait_ge(sem("smin"), 80 * h + 80)
        else:
            eng.wait_ge(sem(f"chin{c % 3}"), due(80 * (3 * h + c // 3) + 80))

    def chunk_load(sp, h, c):
        if c == NCH - 1:
            wait_apart(sp, sem("ul_done"), NCH * h)
        else:
            wait_apart(sp, sem("ul_done"), NCH * h + (c - 3 if c < 3 else c - 2) if not isinstance(h, int) or h > 0 else c - 2)
        n, s = ROWN[c], sem("smin" if c == NCH - 1 else f"chin{c % 3}")
        for i, src in enumerate((q_d, k_d, v_d, ga_d, gb_d)):
            sp.dma_start(chunk_in(c)[:, i, :, 0:n],
                         src[bass.ds(4 * h, 4), :, COL0[c]:COL0[c] + n].rearrange("k p t -> p k t")).then_inc(s, 16)

    def cell_sp(sp, h):
        def state(x, b):
            return x[0, b, bass.ds(h, 1)].rearrange("a (k p) e -> p (a k) e", p=P)

        def state_load(b):
            sp.wait_ge(sem(f"sc_out{b % 2}"), due(64 * h + 16 * (b // 2)))
            sp.dma_start(scs[b % 2][:, :, :], state(a["state_mlstm_c"], b)).then_inc(sem(f"sc_in{b % 2}"), 16)

        def w_load(j):
            sp.wait_ge(sem("o_lo"), due(4 * h + (1 if j == 3 else 0)))
            src = a["mlstm_w_out"][0, bass.ds(MD * h, MD), 256 * j:256 * j + 256]
            sp.dma_start(wraw[j % 3][:, :].rearrange("p (k c) -> p k c", k=4), src.rearrange("(k p) n -> p k n", p=P))\
                .then_inc(sem(f"o_loaded{j % 3}"), 16)

        first = isinstance(h, int) and h == 0
        if not first:
            chunk_load(sp, h, NCH - 1)
        for c in range(3):
            if not first:
                chunk_load(sp, h, c)
            if c == 0:
                sp.wait_ge(sem("w_done"), NCH * h)
                sp.dma_start(abc[:, :], dram(arow_d, ICOL * h + 1, [[0, P], [1, NPR]])).then_inc(sem("abc_in"), 16)
        state_load(0)
        state_load(1)
        for j in range(3):
            w_load(j)
        if first:
            for k in range(KT):
                sp.dma_start(x1T[:, k, :], x1T_d[k]).then_inc(sem("x1_back"), 16)
        for c in range(1, NP):
            b = c - 1
            sp.wait_ge(sem("c_done"), due(NU * h + u_tile(c, True, 3) + 1))
            sp.dma_start(state(o["sample_mlstm_c"], b), scs[b % 2][:, :, :]).then_inc(sem(f"sc_out{b % 2}"), 16)
            if c + 2 < NP:
                chunk_load(sp, h, c + 2)
            if b + 2 < DECB:
                state_load(b + 2)
        w_load(3)
        sp.dma_start(state(o["prompt_mlstm_c"], 0), cst[:, :, :]).then_inc(sem("cst_out"), 16)

    def cell_gp(gp, h):
        def exponents(c):
            n = ROWN[c]
            if c == NCH - 1:
                gp.wait_ge(sem("head_set"), 4 * h + 4)
                gp.tensor_tensor(ees[:, :], habs[:, :], trism[:, :], ALU.add).then_inc(sem("e_ready"), 1)
                return
            gp.wait_ge(sem("abc_in"), 16 * h + 16)
            gp.wait_ge(sem("w_done"), NCH * h + pre_no(c) - 1)
            gp.wait_ge(sem("qs_ready"), NCH * h + pre_no(c))
            gp.tensor_tensor(ee[c % 2][0:n, 0:n], abc[0:n, COL0[c]:COL0[c] + n], tri[0:n, 0:n], ALU.add)\
                .then_inc(sem("e_ready"), 1)

        def queries(c):
            n = ROWN[c]
            if c == NCH - 1:
                gp.wait_ge(sem("smin"), 80 * h + 80)
                w, dst = hws[:, :], qss
            else:
                gp.wait_ge(sem(f"chin{c % 3}"), 80 * (3 * h + c // 3) + 80)
                gp.wait_ge(sem("wint"), NP * h + c + 1)
                gp.wait_ge(sem("u_ready"), used(h, c))
                w, dst = wnt[c % 2][:, 0:n], qs[c % 2]
            if c in (NCH - 1, 0, 1):
                gp.wait_ge(sem("e_ready"), NCH * h + pre_no(c) + 1)
            else:
                gp.wait_ge(sem("kwz_ready"), DECB * h + c - 1)
            gp.tensor_tensor(dst[:, :, 0:n], chunk_in(c)[:, 0, :, 0:n],
                             w.rearrange("p (a t) -> p a t", a=1).to_broadcast([P, 4, n]), ALU.mult)\
                .then_inc(sem("qs_ready"), 1)

        def sequence_keys(b):
            wait_apart(gp, sem("kv_ev"), 2 * NCH * h + 2)
            if b < DECB - 1:
                wait_apart(gp, sem("e_ready"), NCH * h + pre_no(b + 2) + 1)
            else:
                wait_apart(gp, sem("qs_ready"), NCH * h + NCH)
            wait_apart(gp, sem("u_ready"), samp_used(h, b))
            gp.tensor_scalar(kwz[b % 2][:, :], kws[:, :], blkm[:, b:b + 1], None, ALU.mult).then_inc(sem("kwz_ready"), 1)

        exponents(NCH - 1)
        queries(NCH - 1)
        exponents(0)
        queries(0)
        for c in range(NP):
            if c + 1 < NP:
                exponents(c + 1)
            if c >= 1:
                sequence_keys(c - 1)
            if c + 1 < NP:
                queries(c + 1)
        gp.wait_ge(sem("kwz_ready"), DECB * h + DECB)

    def cell_pe(pe, h):
        def pre(c):
            n, x = ROWN[c], chunk_in(c)
            wait_chunk(pe, h, c)
            pe.wait_ge(sem("sw_done"), due(NCH * h + pre_no(c)))
            for k in range(4):
                last = pe.matmul(S_[0:n, 0:n], x[:, 1, k, 0:n], x[:, 0, k, 0:n], start=(k == 0), stop=(k == 3))
            last.then_inc(sem("s_done"), 1)
            pe.wait_ge(sem("kv_ev"), due(2 * NCH * h + 2 * pre_no(c)))
            for i, bank in ((1, KT_), (2, VT_)):
                for k in range(4):
                    last = pe.transpose(bank[0:n, k * P:(k + 1) * P], x[:, i, k, 0:n], ident[:, :])
                last.then_inc(sem("kv_t"), 1)

        def small(z):
            wait_apart(pe, sem("small_read"), NZ * h + z)

        def back(c):
            n = ROWN[c]
            wait_apart(pe, sem("h_done"), NCH * h + c + 1)
            wait_apart(pe, sem("u_mul"), NCH * h + c)
            for k in range(4):
                last = pe.transpose(pm[1][:, k * P:k * P + n], hb[c % 2][0:n, k * P:(k + 1) * P], ident[0:n, 0:n])
            last.then_inc(sem("h_t"), 1)

        if not (isinstance(h, int) and h == 0):
            pe.wait_ge(sem("o_done"), KT * h)
        else:
            pe.wait_ge(sem("col_done"), 1)
        pre(NCH - 1)
        pre(0)
        small(0)
        wait_apart(pe, sem("kv_ev"), 2 * NCH * h + 2)
        for k in range(4):
            pe.matmul(SM[:, DECB * k:DECB * k + DECB], kws[:, k * P:(k + 1) * P], blkm[:, :], start=True, stop=True)
        pe.wait_ge(sem("prod"), h + 1)
        wait_apart(pe, sem("sw_done"), NCH * h + 1)
        for k in range(4):
            pe.matmul(SM[0:NSM, 64:65], prod[:, k, :], ones[:, 0:1], start=(k == 0), stop=False)
        pe.matmul(SM[0:NSM, 64:65], sws[:, :], ones[0:NSM, 0:1], start=False, stop=True).then_inc(sem("small_ready"), 1)

        for c in range(NP):
            n, r = ROWN[c], c % 2
            pe.wait_ge(sem("sw_done"), due(NCH * h + pre_no(c) + 1))
            wait_apart(pe, sem("kv_ev"), 2 * NCH * h + 2 * pre_no(c) + 2)
            pe.wait_ge(sem("h_done"), due(NCH * h + c))
            pe.matmul(pm[0][0:n, :], swb[r][0:n, 0:n], vt[r][0:n, :], start=True, stop=(c == 0))
            small(c + 1)
            pe.matmul(SM[0:n, 0:1], swb[r][0:n, 0:n], ones[0:n, 0:1], start=True, stop=(c == 0))
            if c > 0:
                pe.wait_ge(sem("qs_ready"), due(NCH * h + pre_no(c) + 1))
                pe.wait_ge(sem("c_done"), due(NU * h + u_tile(c - 1, False, 3) + 1))
                for k in range(4):
                    pe.matmul(pm[0][0:n, :], qs[r][:, k, 0:n], cst[:, k, :], start=False, stop=(k == 3))
                    pe.matmul(SM[0:n, 0:1], qs[r][:, k, 0:n], nst[:, k:k + 1], start=False, stop=(k == 3))
            for k in range(4):
                u = u_tile(c, False, k)
                mm = pe.matmul(SM[:, 8 + k:9 + k], kw[r][0:n, k * P:(k + 1) * P], ones[0:n, 0:1], start=True, stop=True)
                if k == 3:
                    mm.then_inc(sem("small_ready"), 1)
                pe.wait_ge(sem("c_done"), due(NU * h + u - 1))
                pe.matmul(U_[u % 2], kw[r][0:n, k * P:(k + 1) * P], vt[r][0:n, :], start=True, stop=True)\
                    .then_inc(sem("u_ready"), 1)
            if c + 1 < NP:
                pre(c + 1)
            if c >= 1:
                b = c - 1
                u = num_tile(b)
                pe.wait_ge(sem(f"sc_in{b % 2}"), 64 * h + 16 * (b // 2) + 16)
                pe.wait_ge(sem("c_done"), NU * h + u - 1)
                for k in range(4):
                    last = pe.matmul(U_[u % 2][0:NSM, :], qss[:, k, :], scs[b % 2][:, k, :], start=(k == 0), stop=(k == 3))
                last.then_inc(sem("u_ready"), 1)
                pe.wait_ge(sem("kwz_ready"), due(DECB * h + b + 1))
                for k in range(4):
                    u = u_tile(c, True, k)
                    pe.wait_ge(sem("c_done"), NU * h + u - 1)
                    pe.matmul(U_[u % 2], kwz[b % 2][:, k * P:(k + 1) * P], vts[:, :], start=True, stop=True)\
                        .then_inc(sem("u_ready"), 1)
            back(c)
        wait_apart(pe, sem("h_done"), NCH * h + NP)
        pe.matmul(pm[0][0:NSM, :], sws[:, :], vts[:, :], start=True, stop=True).then_inc(sem("num9"), 1)
        def out_part(i, groups):
            j, c = i // 2, i % 2
            H = whi[j % 3][:, :].rearrange("p (k m) -> p k m", k=4)
            L = wlo[j % 3][:, :].rearrange("p (k m) -> p k m", k=4)
            for k in range(4):
                for t, (w, x) in enumerate(((H, uh), (H, ul), (L, uh))):
                    for g in groups:
                        last = pe.matmul(ps[i % 2][:, g, 0:GRP], w[:, k, c * P:(c + 1) * P],
                                         x[:, k, g * GRP:(g + 1) * GRP], start=(k == 0 and t == 0), stop=(k == 3 and t == 2))
            return last

        pe.wait_ge(sem("ul_done"), NCH * h + NP)
        pe.wait_ge(sem("c_done"), NU * h + NU)
        pe.wait_ge(sem("o_lo"), 4 * h + 1)
        out_part(0, (0, 1))
        out_part(1, (0, 1))
        back(NCH - 1)
        pe.wait_ge(sem("ul_done"), NCH * h + NCH)
        pe.wait_ge(sem("u_zero"), 2)
        for i in range(2):
            out_part(i, (2,)).then_inc(sem("o_full"), 1)
        for i in range(2, KT):
            pe.wait_ge(sem("o_lo"), 4 * h + i // 2 + 1)
            pe.wait_ge(sem("o_done"), KT * h + i - 1)
            out_part(i, (0, 1, 2)).then_inc(sem("o_full"), 1)

    def cell_act(act, h):
        def weights(c):
            n, r = ROWN[c], c % 2
            sample = c == NCH - 1
            E, W = (ees, sws) if sample else (ee[r], swb[r])
            if sample:
                act.wait_ge(sem("head_set"), 4 * h + 4)
            else:
                act.wait_ge(sem("u_ready"), due(used(h, c)))
                act.wait_ge(sem("abc_in"), 16 * h + 16)
                act.wait_ge(sem("qs_ready"), due(NCH * h + pre_no(c) - 1))
                act.activation(wnt[r][:, 0:n], abc[:, COL0[c]:COL0[c] + n], ACT.Exp, bias=hbc[:, 0, c:c + 1])\
                    .then_inc(sem("wint"), 1)
            act.wait_ge(sem("e_ready"), due(NCH * h + pre_no(c) + 1))
            act.activation(W[0:n, 0:n], E[0:n, 0:n], ACT.Exp, bias=hcol[0:n, c, 0:1]).then_inc(sem("w_done"), 1)

        def turned(c):
            n, r = ROWN[c], c % 2
            K, V = (kws, vts) if c == NCH - 1 else (kw[r], vt[r])
            act.wait_ge(sem("kv_t"), due(2 * NCH * h + 2 * pre_no(c) + 1))
            act.activation(K[0:n, :], KT_[0:n, :], ACT.Copy, scale=hcol[0:n, c, 1:2]).then_inc(sem("kv_ev"), 1)
            act.wait_ge(sem("kv_t"), due(2 * NCH * h + 2 * pre_no(c) + 2))
            act.activation(V[0:n, :], VT_[0:n, :], ACT.Copy).then_inc(sem("kv_ev"), 1)

        def norm(c):
            n, r = ROWN[c], c % 2
            v = cs[0:n, r, 10:11]
            act.wait_ge(sem("var"), due(NCH * h + c + 1))
            act.activation(v, v, ACT.Ln, bias=epsc[0:n, 0:1]).then_inc(sem("h_ln"), 1)
            act.wait_ge(sem("h_ln"), due(NCH * h + c + 1))
            act.activation(v, v, ACT.Exp, scale=-0.5).then_inc(sem("h_rstd"), 1)

        def high(c):
            n, r = ROWN[c], c % 2
            act.wait_ge(sem("u_add"), due(NCH * h + c + 1))
            act.activation(uh[:, :, COL0[c]:COL0[c] + n], ub[r][:, :, 0:n], ACT.Copy).then_inc(sem("uh_done"), 1)

        def w_high(j):
            act.wait_ge(sem(f"o_loaded{j % 3}"), due(32 * h + 16 + 16 * (j // 3) if j % 3 == 0 else 16 * h + 16))
            act.wait_ge(sem("o_full"), due(KT * h + (2 if j == 3 else 0)))
            act.activation(whi[j % 3][:, :], wraw[j % 3][:, :], ACT.Copy).then_inc(sem("o_hi"), 1)

        weights(NCH - 1)
        turned(NCH - 1)
        weights(0)
        turned(0)
        if isinstance(h, int) and h == 0:
            act.wait_ge(sem("orow_out"), 32)
        for c in range(NP):
            if c + 1 < NP:
                weights(c + 1)
                turned(c + 1)
            norm(c)
            if c < 3:
                w_high(c)
            high(c)
        norm(NCH - 1)
        high(NCH - 1)
        w_high(3)

    def cell_dve(dve, h):
        step = [0]

        def done(ins):
            ins.then_inc(sem("cell_step"), 1)
            step[0] += 1
            wait_apart(dve, sem("cell_step"), CELL_STEPS * h + step[0])

        def scores(c):
            n, r = ROWN[c], c % 2
            W = sws if c == NCH - 1 else swb[r]
            dve.wait_ge(sem("s_done"), due(NCH * h + pre_no(c) + 1))
            dve.wait_ge(sem("w_done"), due(NCH * h + pre_no(c) + 1))
            dve.tensor_tensor(W[0:n, 0:n], S_[0:n, 0:n], W[0:n, 0:n], ALU.mult).then_inc(sem("sw_done"), 1)

        def small(z):
            dve.wait_ge(sem("small_ready"), due(NZ * h + z + 1))

        def numerator(c):
            return nums[:, :] if c == NCH - 1 else pm[0][0:ROWN[c], :]

        def statistics(c):
            n, r = ROWN[c], c % 2
            x = cs[0:n, r, :]
            done(dve.scalar_tensor_tensor(x[:, 1:2], x[:, 0:1], -1.0, x[:, 0:1], ALU.mult, ALU.max))
            done(dve.tensor_tensor(x[:, 1:2], x[:, 1:2], hcol[0:n, c, 2:3], ALU.max))
            dve.reciprocal(x[:, 1:2], x[:, 1:2])
            done(dve.bn_stats(x[:, 2:8], numerator(c)))
            done(dve.bn_aggr(x[:, 8:10], x[:, 2:8]))
            dve.tensor_scalar(x[:, 10:11], x[:, 9:10], x[:, 1:2], x[:, 1:2], ALU.mult, ALU.mult).then_inc(sem("var"), 1)

        def normed(c):
            n, r = ROWN[c], c % 2
            x = cs[0:n, r, :]
            dve.wait_ge(sem("h_rstd"), due(NCH * h + c + 1))
            done(dve.tensor_tensor(x[:, 11:12], x[:, 10:11], x[:, 1:2], ALU.mult))
            dve.tensor_scalar(hb[r][0:n, :], numerator(c), x[:, 8:9], x[:, 11:12], ALU.subtract, ALU.mult)\
                .then_inc(sem("h_done"), 1)

        def put(c):
            n, r = ROWN[c], c % 2
            x, u = chunk_in(c), ub[r]
            dve.wait_ge(sem("h_t"), due(NCH * h + c + 1))
            dve.tensor_tensor(u[:, :, 0:n], pm[1][:, :].rearrange("p (k t) -> p k t", k=4)[:, :, 0:n], x[:, 3, :, 0:n], ALU.mult)\
                .then_inc(sem("u_mul"), 1)
            dve.wait_ge(sem("u_mul"), due(NCH * h + c + 1))
            dve.tensor_tensor(u[:, :, 0:n], u[:, :, 0:n], x[:, 4, :, 0:n], ALU.add).then_inc(sem("u_add"), 1)
            dve.wait_ge(sem("uh_done"), due(NCH * h + c + 1))
            cols = slice(COL0[c], COL0[c] + n)
            dve.tensor_tensor(ul[:, :, cols], u[:, :, 0:n], uh[:, :, cols].bitcast(F32), ALU.subtract).then_inc(sem("ul_done"), 1)

        def w_low(j):
            dve.wait_ge(sem("o_hi"), due(4 * h + j + 1))
            dve.tensor_tensor(wlo[j % 3][:, :], wraw[j % 3][:, :], whi[j % 3][:, :].bitcast(F32), ALU.subtract)\
                .then_inc(sem("o_lo"), 1)

        if isinstance(h, int) and h == 0:
            dve.wait_ge(sem("col_done"), 1)
            dve.wait_ge(sem("rows_in"), 96)
        dve.tensor_copy(hcol[:, :, :].rearrange("p c (x a) -> p c x a", a=1),
                        col[:, :, :].rearrange("p c (x y) -> p c x y", x=4)[:, :, 0:3, bass.ds(h, 1)]).then_inc(sem("head_set"), 1)
        dve.tensor_copy(hbc[:, :, :], bcs[:, :, bass.ds(h, 1), :].rearrange("p x a c -> p (x a) c")).then_inc(sem("head_set"), 1)
        dve.tensor_copy(hws[:, :], wsb[:, bass.ds(h, 1), :].rearrange("p a c -> p (a c)")).then_inc(sem("head_set"), 1)
        dve.tensor_copy(habs[:, :], absm[:, bass.ds(h, 1), :].rearrange("p a c -> p (a c)")).then_inc(sem("head_set"), 1)
        dve.wait_ge(sem("head_set"), 4 * h + 4)
        snh = sn[:, :, :].rearrange("p k (b h) -> p k b h", h=MH)[:, :, :, bass.ds(h, 1)]
        snwh = snew[:, :, :].rearrange("p k (b h) -> p k b h", h=MH)[:, :, :, bass.ds(h, 1)]
        dve.wait_ge(sem("qs_ready"), NCH * h + 1)
        dve.tensor_tensor(prod[:, :, :].rearrange("p k (b t) -> p k b t", b=DECB),
                          qss[:, :, :].rearrange("p k (b t) -> p k b t", b=DECB),
                          snh.to_broadcast([P, 4, DECB, DECT]), ALU.mult).then_inc(sem("prod"), 1)
        scores(NCH - 1)
        scores(0)
        small(0)
        done(dve.tensor_tensor(ntmp[:, :, :].rearrange("p k (b a) -> p k b a", a=1), snh,
                               hbc[:, 1, NP:].rearrange("p (k b a) -> p k b a", k=1, a=1).to_broadcast([P, 4, DECB, 1]), ALU.mult))
        dve.tensor_copy(cs[0:NSM, 1, 12:13], SM[0:NSM, 64:65])
        done(dve.tensor_tensor(snwh, ntmp[:, :, :].rearrange("p k (b a) -> p k b a", a=1),
                               SM[:, 0:4 * DECB].rearrange("p (k b a) -> p k b a", k=4, a=1), ALU.add))
        dve.sem_inc(sem("small_read"), 1)
        for c in range(NP):
            n, r = ROWN[c], c % 2
            if c == 0:
                dve.wait_ge(sem("cst_out"), 16 * h)
            for k in range(4):
                dve.wait_ge(sem("u_ready"), due(NU * h + u_tile(c, False, k) + 1))
                U = U_[u_tile(c, False, k) % 2]
                if c == 0:
                    ins = dve.tensor_copy(cst[:, k, :], U)
                else:
                    ins = dve.scalar_tensor_tensor(cst[:, k, :], cst[:, k, :], hbc[:, 1, c:c + 1], U, ALU.mult, ALU.add)
                ins.then_inc(sem("c_done"), 1)
            small(c + 1)
            if c == 0:
                dve.tensor_copy(nst[:, :], SM[:, 8:12])
            else:
                dve.scalar_tensor_tensor(nst[:, :], nst[:, :], hbc[:, 1, c:c + 1], SM[:, 8:12], ALU.mult, ALU.add)
            done(dve.tensor_copy(cs[0:n, r, 0:1], SM[0:n, 0:1]))
            dve.sem_inc(sem("small_read"), 1)
            if c + 1 < NP:
                scores(c + 1)
            statistics(c)
            if c == 0:
                normed(c)
            else:
                b = c - 1
                u = num_tile(b)
                dve.wait_ge(sem("u_ready"), NU * h + u + 1)
                dve.wait_ge(sem("num_add"), DECB * h + b)
                if b == 0:
                    ins = dve.tensor_scalar(nums[:, :], U_[u % 2][0:NSM, :], blkm[:, b:b + 1], None, ALU.mult)
                else:
                    ins = dve.scalar_tensor_tensor(nums[:, :], U_[u % 2][0:NSM, :], blkm[:, b:b + 1], nums[:, :],
                                                   ALU.mult, ALU.add)
                ins.then_inc(sem("num_add"), 1)
                dve.wait_ge(sem("num_add"), DECB * h + b + 1)
                dve.sem_inc(sem("c_done"), 1)
                for k in range(4):
                    dve.wait_ge(sem("u_ready"), due(NU * h + u_tile(c, True, k) + 1))
                    u = u_tile(c, True, k)
                    dve.scalar_tensor_tensor(scs[b % 2][:, k, :], scs[b % 2][:, k, :], hbc[:, 1, NP + b:NP + b + 1], U_[u % 2],
                                             ALU.mult, ALU.add).then_inc(sem("c_done"), 1)
                    if k == 1:
                        normed(c)
            put(c)
            if c < 3:
                w_low(c)
        done(dve.tensor_copy(cs[0:NSM, 1, 0:1], cs[0:NSM, 1, 12:13]))
        dve.tensor_copy(nall[:, bass.ds(h, 1), :].rearrange("p a k -> p (a k)"), nst[:, :])
        dve.wait_ge(sem("num9"), h + 1)
        done(dve.tensor_tensor(nums[:, :], nums[:, :], pm[0][0:NSM, :], ALU.add))
        statistics(NCH - 1)
        normed(NCH - 1)
        put(NCH - 1)
        if isinstance(h, int) and h == 0:
            dve.wait_ge(sem("x1_back"), 16 * KT)
        for i in range(KT):
            dve.wait_ge(sem("o_full"), KT * h + i + 1)
            dve.tensor_tensor(v3(x1T[:, i, :]), ps[i % 2][:, :, 0:GRP], v3(x1T[:, i, :]), ALU.add).then_inc(sem("o_done"), 1)
            if i == 1:
                w_low(3)
        dve.wait_ge(sem("o_done"), KT * h + KT)
        assert step[0] == CELL_STEPS, step[0]

    def final_pe(pe):
        pe.wait_ge(sem("o_done"), KT * MH)
        for k in range(4):
            pe.transpose(pm[0][0:32, k * P:(k + 1) * P], snew[:, k, :], ident[:, :])
        pe.transpose(pm[1][0:4 * MH, 0:P], nall[:, :, :].rearrange("p h k -> p (h k)"), ident[:, :]).then_inc(sem("n_t"), 1)
        for i in range(NBLK + 1):
            c, n = COL0[i + 1], ROWN[i + 1]
            pe.wait_ge(sem("y_ev"), due(i - 1))
            for j in range(KT):
                last = pe.transpose(ps[i % 2][0:n, j // 4, (j % 4) * P:(j % 4) * P + P], x1T[:, j, c:c + n], ident[:, :])
            last.then_inc(sem("y_t"), 1)

    def final_dve(dve):
        dve.wait_ge(sem("n_t"), 1)
        dve.tensor_copy(snin[:, :], pm[0][0:32, :]).then_inc(sem("n_ev"), 1)
        dve.tensor_copy(nrow4[:, :], pm[1][0:4 * MH, 0:P]).then_inc(sem("n_ev"), 1)
        dve.wait_ge(sem("sc_out0"), 64 * MH)
        dve.wait_ge(sem("sc_out1"), 64 * MH)
        dve.wait_ge(sem("cst_out"), 16 * MH)
        for i in range(NBLK + 1):
            n = ROWN[i + 1]
            dve.wait_ge(sem("y_t"), i + 1)
            dve.wait_ge(sem(f"y_out{i % 2}"), 16 * (i // 2))
            dve.tensor_copy(ytok[i % 2][0:n, :].rearrange("p (g c) -> p g c", g=2), ps[i % 2][0:n, 0:2, :])\
                .then_inc(sem("y_ev"), 1)

    def final_sp(sp):
        sp.wait_ge(sem("n_ev"), 2)
        sp.dma_start(o["sample_mlstm_n"][0].rearrange("b h d -> (b h) d"), snin[:, :]).then_inc(sem("out"), 16)
        sp.dma_start(o["prompt_mlstm_n"][0, 0].rearrange("h (k p) -> (h k) p", p=P), nrow4[:, :]).then_inc(sem("out"), 16)
        for i in range(NBLK + 1):
            sp.wait_ge(sem("y_ev"), i + 1)
            dst = o["y_prompt"][0, P * i:P * (i + 1), :] if i < NBLK else o["y_sample"].rearrange("b t d -> (b t) d")
            sp.dma_start(dst, ytok[i % 2][0:ROWN[i + 1], :]).then_inc(sem(f"y_out{i % 2}"), 16)
        sp.wait_ge(sem("out"), 32)
        sp.wait_ge(sem("y_out0"), 16 * 5)
        sp.wait_ge(sem("y_out1"), 16 * 4)
        sp.wait_ge(sem("cst_out"), 16 * MH)
        sp.wait_ge(sem("sc_out0"), 64 * MH)
        sp.wait_ge(sem("sc_out1"), 64 * MH)
        sp.wait_ge(sem("orow_out"), 32)


    w_out0 = a["swa_w_out"][0].rearrange("(k p) n -> p k n", p=P)

    with nc.Block() as block:

        @block.sync
        def _(sp):
            for dst, src in ((ident, "c_ident"), (headsum, "c_headsum"), (onehot, "c_onehot"), (headsel, "c_headsel")):
                sp.dma_start(dst[:, :], a[src]).then_inc(sem("consts"), 16)
            sp.dma_start(crow[:, :], a["state_mlstm_conv"][0].rearrange("b w c -> (b w) c")).then_inc(sem("consts"), 16)
            for n in range(NTT):
                sp.wait_ge(sem("xt_t"), due(n - 2))
                for src, r0, nr in input_parts(n):
                    sp.dma_start(xtok[n % 3][r0:r0 + nr, :], src).then_inc(sem(f"xtok{n % 3}"), 16)
            for n in range(3):
                slot_load(sp, Idx(n), w_in0[:, :, in_order[n]:in_order[n] + P], KT)
            sp.wait_ge(sem("xt_ev"), NTT)
            for k in range(KT):
                sp.dma_start(xT_d[k], xT[:, k, :]).then_inc(sem("xT_saved"), 16)
            for n in range(3, NS0):
                slot_load(sp, Idx(n), w_in0[:, :, in_order[n]:in_order[n] + P], KT)
            for n in range(NS0, NS0 + 3):
                slot_load(sp, Idx(n), w_out0[:, :, (n - NS0) * P:(n - NS0 + 1) * P], KT)
            sp.wait_ge(sem("ps_full"), NS0)
            sp.wait_ge(sem("rel_saved"), 16)
            sp.dma_start(bias[:, :, 2 * P:KEYS], dram(rel_d, RBAND + P - 1, [[RROW, P], [HREL, NH], [1, META]]))\
                .then_inc(sem("bias_in"), 16)
            sp.dma_start(bias[:, :, P:2 * P], dram(rel_d, 2 * P - 1, [[RROW, P], [HREL, NH], [1, P]]))\
                .then_inc(sem("bias_in"), 16)
            sp.dma_start(sinkb[:, :], dram(a["swa_sinks"], 0, [[0, P], [1, NH]])).then_inc(sem("bias_in"), 16)
            sp.wait_ge(sem("hn_done"), 10)

            def k_load(dst, sem_, c):
                sp.dma_start(dst[:, :, 0, :], kqv[:, 0:2, c]).then_inc(sem_, 16)
                sp.dma_start(dst[0:64, :, 1, :], kqv[64:128, 0:2, c]).then_inc(sem_, 16)
                sp.dma_start(dst[64:128, :, 1, :], kqv[0:64, 0:2, c]).then_inc(sem_, 16)

            for i in range(2):
                k_load(kb[i][:, :, :, P:P + META], sem("km_in"), slice(0, META))
            k_load(kb[1][:, :, :, 0:P], sem("km_in"), slice(META, META + P))

            def blk_load(b):
                q = b.mod(2)
                if not (isinstance(b.v, int) and b.v == 0):
                    sp.wait_ge(sem("s_ready"), due(4 * b.v))
                c = bass.ds(META + b.v * P, P)
                sp.dma_start(qb[q][:, :, :], kqv[:, 2:10, c]).then_inc(sem(f"blk{q}"), 16)
                k_load(kb[q][:, :, :, 0:P], sem(f"blk{q}"), c)

            blk_load(Idx(0))
            sp.wait_ge(sem("tk_copied"), 1)
            sp.wait_ge(sem("g_attn"), 3)
            for g in range(4):
                sp.dma_start(vbd[META * g:META * g + META, :, 64 * g:64 * g + 64],
                             vtok[0:META, 0, :].rearrange("k (h d) -> k h d", h=KVH)).then_inc(sem("vbd_in"), 16)
            sp.wait_ge(sem("biased"), 8)
            sp.dma_start(bias[:, :, 2 * P:KEYS], dram(rel_d, RBAND + RMETA, [[0, P], [HREL, NH], [1, META]]))\
                .then_inc(sem("bias_in"), 16)
            sp.dma_start(bias[:, :, 0:P], dram(rel_d, P - 1, [[RROW, P], [HREL, NH], [1, P]]))\
                .then_inc(sem("bias_in"), 16)
            blk_load(Idx(1))
            sweep(sp, 2, 6, 2, blk_load, peel=0)
            sp.wait_ge(sem("g_attn"), 8)
            for H in range(NH):
                r = 32 * (H // 4) + DECT * (H % 4)
                sp.dma_start(biasS[r:r + DECT, 0:META], dram(rel_d, H * HREL + RBAND + RMETA, [[0, DECT], [1, META]]))\
                    .then_inc(sem("sa_bias"), 16)
                sp.dma_start(biasS[r:r + DECT, META:SKEYS], dram(rel_d, H * HREL + P - 1, [[RROW, DECT], [1, SKEYS - META]]))\
                    .then_inc(sem("sa_bias"), 16)
            sp.wait_ge(sem("tk_copied"), len(TURNS))
            sp.dma_start(vnew_d.rearrange("b t c -> (b t) c"), vtok[0:NSM, NBLK + 1, :]).then_inc(sem("vnew"), 16)
            sp.dma_start(knew_d.rearrange("b t c -> (b t) c"), ktok[0:NSM, 2, :]).then_inc(sem("knew"), 16)
            sp.wait_ge(sem("vnew"), 16)
            sp.wait_ge(sem("knew"), 16)
            for name, tok, last, src in (("k", ktok, 1, knew_d), ("v", vtok, NBLK, vnew_d)):
                sp.dma_start(o[f"prompt_swa_{name}"][0, 0].rearrange("t h d -> t (h d)"), tok[:, last, :])\
                    .then_inc(sem("l0_out"), 16)
                sp.dma_start(o[f"prompt_swa_meta_{name}"][0, 0].rearrange("t h d -> t (h d)"), tok[0:META, 0, :])\
                    .then_inc(sem("l0_out"), 16)
                cache = o[f"sample_swa_{name}"][0].rearrange("b t h d -> b t (h d)")
                old = a[f"cache_swa_{name}"][0].rearrange("b t h d -> b t (h d)")
                sp.dma_start(cache[:, WIN - DECT:WIN, :], src).then_inc(sem("l0_out"), 16)
                sp.dma_start(cache[:, 0:WIN - DECT, :], old[:, DECT:WIN, :]).then_inc(sem("l0_out"), 16)
            sweep(sp, 0, DECB, 2, lambda b: samp_loads(sp, b), peel=1)
            sp.wait_ge(sem("sa_lo"), 1)
            for j in range(KT):
                n = NS0 + 3 + j
                if n < NS0 + NS1:
                    slot_load(sp, Idx(n), w_out0[:, :, (n - NS0) * P:(n - NS0 + 1) * P], KT)
                else:
                    slot_load(sp, Idx(n), *p1_source(0, n - NS0 - NS1))
                sp.wait_ge(sem("x1_done"), due(j - 1))
                sp.dma_start(xres[j % 2][:, 0, :], xT_d[j]).then_inc(sem(f"xres{j % 2}"), 16)
            for j in range(KT):
                sp.wait_ge(sem("x1_done"), due(j + 1))
                sp.dma_start(x1T_d[j], x1T[:, j, :]).then_inc(sem("x1_saved"), 16)
            heads(sp, p1_sp)
            for t, c in (("st0_out", 64), ("st1_out", 128), ("st2_out", 128)):
                sp.wait_ge(sem(t), due(c * MH))
            sp.wait_ge(sem("l0_out"), 16 * 8)

        @block.gpsimd
        def _(gp):
            gp.memset(ones[:, :], 1.0).then_inc(sem("g_const"), 1)
            gp.memset(epsc[:, :], EPS).then_inc(sem("g_const"), 1)
            gp.memset(xT[:, :, T:TP], 0.0).then_inc(sem("g_const"), 1)
            gp.wait_ge(sem("g_const"), 3)
            gp.memset(relb[NBK:NBK + 1, :], NEG).then_inc(sem("g_const"), 1)
            gp.wait_ge(sem("ps_full"), NS0)
            gp.memset(bias[:, :, 0:P], NEG).then_inc(sem("g_attn"), 1)
            gp.memset(vtok[:, 0, :], 0.0).then_inc(sem("g_attn"), 1)
            gp.memset(vbd[:, :, :], 0.0).then_inc(sem("g_attn"), 1)
            gp.wait_ge(sem("g_const"), 4)
            gp.wait_ge(sem("g_attn"), 3)
            gp.wait_ge(sem("hn_done"), 10)
            for t in (qsb[0], qsb[1]):
                gp.memset(t[:, :, :], 0.0).then_inc(sem("g_attn"), 1)
            gp.wait_ge(sem("g_attn"), 5)
            gp.memset(biasS[:, :], 0.0).then_inc(sem("g_attn"), 1)
            gp.memset(oh[:, :, T:TP].bitcast(F32), 0.0).then_inc(sem("g_attn"), 1)
            gp.memset(ol[:, :, T:TP].bitcast(F32), 0.0).then_inc(sem("g_attn"), 1)
            sweep(gp, 0, UNITS, 8, lambda s: att_pack(gp, s), peel=1)
            gp.wait_ge(sem("x1_done"), 1)
            gp.memset(wg[:, :, :], 0.0).then_inc(sem("g_conv"), 1)
            gp.wait_ge(sem("rms_lo"), 2 * KT)
            for i in range(2):
                gp.memset(xr[i][:, 0:CW - 1], 0.0).then_inc(sem("g_conv"), 1)
                gp.memset(xc[i][:, 0, T:TP], 0.0).then_inc(sem("g_conv"), 1)
            heads(gp, p1_gp)

        @block.tensor
        def _(pe):
            pe.wait_ge(sem("consts"), 16 * 16)
            pe.wait_ge(sem("g_const"), 4)
            pe.transpose(pm[0][:, 0:P], vrow[:, :], ident[:, :])
            pe.transpose(pm[0][:, P:P + 2], nrow[:, :], ident[0:2, 0:2])
            pe.matmul(pm[0][:, 130:131], headsel[:, :], sinkc[:, :], start=True, stop=True)
            pe.matmul(pm[0][0:NH, 160:160 + RROW - RBAND], relb[:, :], onehot[:, RBAND:RROW], start=True, stop=True)
            pe.matmul(pm[1][0:NH, 0:RBAND], relb[:, :], onehot[:, 0:RBAND], start=True, stop=True)\
                .then_inc(sem("vec_t"), 1)
            for n in range(NTT):
                pe.wait_ge(sem(f"xtok{n % 3}"), due(sum(16 * len(input_parts(m)) for m in range(n % 3, n + 1, 3))))
                pe.wait_ge(sem("xt_ev"), due(n - 1))
                r = rows_of[n]
                for j in range(KT):
                    last = pe.transpose(ps[n % 2][:, j // 4, (j % 4) * P:(j % 4) * P + r],
                                        xtok[n % 3][0:r, j * P:(j + 1) * P], ident[0:r, 0:r])
                last.then_inc(sem("xt_t"), 1)
            pe.wait_ge(sem("xt_ev"), NTT)
            rms_pe(pe, 0)
            pe.wait_ge(sem("vcols"), 5)
            for k in range(16):
                last = pe.transpose(pm[1][:, 24 * k:24 * k + 24], crow[:, k * P:(k + 1) * P], ident[0:24, 0:24])
            last.then_inc(sem("ctx_t"), 1)

            def in_step(n):
                hn = None
                if isinstance(n.v, int) and n.v >= 10:
                    m = n + (-10)
                    hn_pe(pe, m, 0)
                    hn_pe(pe, m, 1)
                    hn = lambda: hn_pe(pe, m, 2)
                product(pe, n, n, KT, 0, hh, hl, hn, 0 if isinstance(n.v, int) and n.v == 0 else None)

            sweep(pe, 0, 10, 6, in_step, peel=0)
            pe.wait_ge(sem("ctx_kept"), 1)
            sweep(pe, 10, 10, 6, in_step, peel=0)
            pe.wait_ge(sem("ps_free0"), NS0 // 2)
            pe.wait_ge(sem("ps_free1"), NS0 // 2)
            pe.wait_ge(sem("hn_done"), 10)
            turn_pe(pe)
            pe.wait_ge(sem("tk_copied"), len(TURNS))
            pe.wait_ge(sem("km_in"), 144)
            att_scores(pe, Idx(0))
            att_scores(pe, Idx(1))
            pe.wait_ge(sem("vbd_in"), 64)

            def att_step(s):
                att_turn(pe, s)
                if not (isinstance(s.v, int) and s.v == 0):
                    att_out_turn(pe, s + (-1))
                if not (isinstance(s.v, int) and s.v + 2 >= UNITS):
                    att_scores(pe, s + 2)
                att_values(pe, s)

            sweep(pe, 0, UNITS, 8, att_step, peel=1, tail=1)
            att_out_turn(pe, Idx(UNITS - 1))
            meta_pe(pe)
            pe.wait_ge(sem("m_lo"), 1)
            pe.wait_ge(sem("sa_bias"), 16 * 2 * NH)

            def samp_step(b):
                samp_turn(pe, b)
                more = not (isinstance(b.v, int) and b.v + 1 >= DECB)
                if more:
                    samp_turn_keys(pe, b + 1)
                samp_values(pe, b)
                if more:
                    samp_scores(pe, b + 1)
                samp_out_turn(pe, b)

            samp_turn_keys(pe, Idx(0))
            samp_scores(pe, Idx(0))
            sweep(pe, 0, DECB, 2, samp_step, peel=1, tail=1)
            pe.wait_ge(sem("sa_lo"), 1)
            for n in range(NS0, NS0 + NS1):
                product(pe, Idx(n), Idx(n), KT, 0, oh, ol)
            pe.wait_ge(sem("ps_free0"), L1T // 2)
            rms_pe(pe, 1)
            pe.wait_ge(sem("g_conv"), 1)
            for g in range(3):
                r = 64 if g == 1 else 0
                last = pe.matmul(pm[g // 2][r:r + 36, 0:GRP], wg[:, 0, :], x1T[:, 0, 0:GRP], start=True, stop=False,
                                 skip_group_check=True)
            last.then_inc(sem("gate_zero"), 1)
            heads(pe, p1_pe)
            pe.wait_ge(sem("tail_saved"), 16)
            pe.wait_ge(sem("ps_free0"), (L1T + MH * HT) // 2)
            pe.wait_ge(sem("ps_free1"), (L1T + MH * HT) // 2)
            for q in range(4):
                for k in range(4):
                    last = pe.transpose(ps[q // 2][0:27, q % 2, k * P:(k + 1) * P], ctail[:, 4 * q + k, :], ident[:, :])
                last.then_inc(sem("tail_t"), 1)

        @block.scalar
        def _(act):
            for r, n, v in ((0, 16, a["norm_w"].rearrange("l (k p) -> (l k) p", p=P)),
                            (16, 64, a["mlstm_conv_w"][0].rearrange("w (k p) -> (w k) p", p=P)),
                            (80, 16, a["mlstm_conv_b"].rearrange("l (k p) -> (l k) p", p=P)),
                            (96, 16, a["mlstm_head_norm"].rearrange("l (k p) -> (l k) p", p=P)),
                            (112, 16, a["mlstm_skip"].rearrange("l (k p) -> (l k) p", p=P))):
                act.dma_start(vrow[r:r + n, :], v).then_inc(sem("consts"), 16)
            for h in range(2):
                act.dma_start(nrow[0:1, 64 * h:64 * h + 64], a["swa_k_norm"]).then_inc(sem("consts"), 16)
                act.dma_start(nrow[1:2, 64 * h:64 * h + 64], a["swa_q_norm"]).then_inc(sem("consts"), 16)
            act.dma_start(relb[0:NBK, :], a["rel_bias"]).then_inc(sem("consts"), 16)
            act.dma_start(sinkc[:, :], dram(a["swa_sinks"], 0, [[1, NH], [1, 1]])).then_inc(sem("consts"), 16)
            act.wait_ge(sem("vcols"), 5)
            act.dma_start(dram(rel_d, 0, [[HREL, NH], [RROW + 1, P], [1, RROW]]),
                          rtab[:, :].rearrange("h (a u) -> h a u", a=1).to_broadcast([NH, P, RROW])).then_inc(sem("rel_saved"), 16)
            act.wait_ge(sem("g_const"), 4)
            for n in range(3):
                split_hi(act, Idx(n), 0)
            rms_act(act, xT, hh, 0, (sem("xt_ev"), lambda k: NTT))
            act.wait_ge(sem("xT_saved"), 16 * KT)
            act.wait_ge(sem("rms_lo"), KT)

            def in_step(n, kind):
                if kind > 0:
                    hn_act(act, n + (-10))
                s = n.mod(2)
                act.wait_ge(sem("ps_full"), due(n + 1))
                dst = kqv[:, bass.ds(n.v, 1), :] if kind < 2 else gate[:, bass.ds(n.v - 12, 1), :]
                act.activation(dst.rearrange("p a (g c) -> p (a g) c", g=3), ps[s][:, :, 0:GRP],
                               ACT.Copy if kind < 2 else ACT.Silu).then_inc(sem(f"ps_free{s}"), 1)
                split_hi(act, n + 3, n + 1)
                if isinstance(n.v, int) and 9 <= n.v < 19:
                    hn_square(act, n + (-9))

            sweep(act, 0, 9, 6, lambda n: in_step(n, 0), peel=0)
            in_step(Idx(9), 0)
            sweep(act, 10, 2, 6, lambda n: in_step(n, 1), peel=0)
            sweep(act, 12, 8, 6, lambda n: in_step(n, 2), peel=0)

            def att_step(s):
                att_turned_act(act, s)
                if not (isinstance(s.v, int) and s.v == 0):
                    att_high(act, s + (-1))
                if not (isinstance(s.v, int) and s.v + 2 >= UNITS):
                    att_exp(act, s + 2)

            att_exp(act, Idx(0))
            att_exp(act, Idx(1))
            sweep(act, 0, UNITS, 8, att_step, peel=1, tail=1)
            att_high(act, Idx(UNITS - 1))
            meta_act(act)
            def samp_step(b):
                samp_turned_act(act, b)
                if not (isinstance(b.v, int) and b.v + 1 >= DECB):
                    samp_keys_act(act, b + 1)
                    samp_exp(act, b + 1)

            samp_keys_act(act, Idx(0))
            samp_exp(act, Idx(0))
            sweep(act, 0, DECB, 2, samp_step, peel=1, tail=1)
            act.wait_ge(sem("sa_gated"), DECB)
            act.activation(oh[:, :, NPR:T], ogS[:, :, :], ACT.Copy).then_inc(sem("sa_hi"), 1)
            for n in range(NS0, NS0 + NS1):
                split_hi(act, Idx(n + 3), n + 1)
            rms_act(act, x1T, h1h, 1, (sem("x1_done"), lambda k: k + 1))
            act.wait_ge(sem("x1_saved"), 16 * KT)
            act.wait_ge(sem("gate_zero"), 1)
            act.wait_ge(sem("g_conv"), 5)
            heads(act, p1_act)

        @block.vector
        def _(dve):
            dve.wait_ge(sem("vec_t"), 1)
            dve.tensor_copy(vcol[:, :], pm[0][:, 0:P]).then_inc(sem("vcols"), 1)
            dve.tensor_copy(qkw[:, :], pm[0][:, P:P + 2]).then_inc(sem("vcols"), 1)
            dve.tensor_copy(sinkv[:, 0:1], pm[0][:, 130:131]).then_inc(sem("vcols"), 1)
            dve.tensor_copy(rtab[:, RBAND:RROW], pm[0][0:NH, 160:160 + RROW - RBAND]).then_inc(sem("vcols"), 1)
            dve.tensor_copy(rtab[:, 0:RBAND], pm[1][0:NH, 0:RBAND]).then_inc(sem("vcols"), 1)
            for n in range(NTT):
                dve.wait_ge(sem("xt_t"), due(n + 1))
                r = rows_of[n]
                dve.tensor_copy(xT[:, :, n * P:n * P + r],
                                ps[n % 2][:, 0:2, :].rearrange("p g (j c) -> p (g j) c", c=P)[:, :, 0:r])\
                    .then_inc(sem("xt_ev"), 1)
            dve.wait_ge(sem("vcols"), 5)
            for n in range(3):
                split_lo(dve, Idx(n))
            rms_dve(dve, xT, hh, hl, 0, 0)
            dve.wait_ge(sem("ctx_t"), 1)
            dve.wait_ge(sem("rel_saved"), 16)
            dve.tensor_copy(cstate[:, :, :].rearrange("p k c -> p (k c)"), pm[1][:, 0:384]).then_inc(sem("ctx_kept"), 1)
            def in_step(n):
                split_lo(dve, n + 3)
                if isinstance(n.v, int) and n.v >= 10:
                    hn_dve(dve, n + (-10))

            sweep(dve, 0, 10, 6, in_step, peel=0)
            sweep(dve, 10, 10, 6, in_step, peel=0)
            dve.wait_ge(sem("g_attn"), 3)
            turn_dve(dve)
            dve.wait_ge(sem("bias_in"), 48)
            dve.tensor_scalar(nsink[:, :], sinkb[:, :], -1.0, None, ALU.mult).then_inc(sem("nsink"), 1)
            dve.tensor_copy(sinks[:, 0:1], sinkv[:, 0:1]).then_inc(sem("nsink"), 1)
            dve.tensor_scalar(sinks[:, 1:2], sinkv[:, 0:1], -1.0, None, ALU.mult).then_inc(sem("nsink"), 1)
            dve.wait_ge(sem("nsink"), 3)
            att_softmax_dve(dve, Idx(0))
            att_softmax_dve(dve, Idx(1))

            def att_step(s):
                att_turned_dve(dve, s)
                if not (isinstance(s.v, int) and s.v == 0):
                    att_gate(dve, s + (-1))
                if not (isinstance(s.v, int) and s.v + 2 >= UNITS):
                    if isinstance(s.v, int) and s.v + 2 == 4:
                        dve.wait_ge(sem("bias_in"), 80)
                    att_softmax_dve(dve, s + 2)
                att_out_dve(dve, s)
                if not (isinstance(s.v, int) and s.v == 0):
                    att_low(dve, s + (-1))

            sweep(dve, 0, UNITS, 8, att_step, peel=1, tail=1)
            att_gate(dve, Idx(UNITS - 1))
            att_low(dve, Idx(UNITS - 1))
            meta_dve(dve)
            dve.wait_ge(sem("sa_bias"), 16 * 2 * NH)

            def samp_step(b):
                more = not (isinstance(b.v, int) and b.v + 1 >= DECB)
                if more:
                    samp_queries_dve(dve, b + 1)
                samp_out_dve(dve, b)
                if more:
                    samp_softmax_dve(dve, b + 1)
                samp_gate(dve, b)

            samp_queries_dve(dve, Idx(0))
            samp_softmax_dve(dve, Idx(0))
            sweep(dve, 0, DECB, 2, samp_step, peel=1, tail=1)
            dve.wait_ge(sem("sa_hi"), 1)
            dve.tensor_tensor(ol[:, :, NPR:T], ogS[:, :, :], oh[:, :, NPR:T].bitcast(F32), ALU.subtract)\
                .then_inc(sem("sa_lo"), 1)
            dve.wait_ge(sem("l0_out"), 16 * 8)
            for j in range(KT):
                split_lo(dve, Idx(NS0 + 3 + j))
                dve.wait_ge(sem("ps_full"), due(NS0 + j + 1))
                dve.wait_ge(sem(f"xres{j % 2}"), due(16 * (j // 2) + 16))
                dve.tensor_tensor(v3(x1T[:, j, :]), ps[j % 2][:, :, 0:GRP], v3(xres[j % 2][:, 0, :]), ALU.add)\
                    .then_inc(sem("x1_done"), 1)
                dve.wait_ge(sem("x1_done"), due(j + 1))
                dve.sem_inc(sem(f"ps_free{j % 2}"), 1)
            rms_dve(dve, x1T, h1h, h1l, 1, 1)
            heads(dve, p1_dve)
            dve.wait_ge(sem("ps_full"), L1T + MH * HT)
            for q in range(4):
                dve.wait_ge(sem("tail_t"), due(q + 1))
                dve.tensor_copy(orow[:, q * 512:(q + 1) * 512], ps[q // 2][0:27, q % 2, :]).then_inc(sem("orow_done"), 1)

    nc.clear_and_free_semaphores(list(sems.values()))
    nc.all_engine_barrier()
    sems.clear()
    sem_suffix[0] = "_cell"

    with nc.Block() as block:

        @block.sync
        def _(sp):
            gates_sp(sp)
            heads(sp, cell_sp)
            final_sp(sp)

        @block.gpsimd
        def _(gp):
            gates_gp(gp)
            heads(gp, cell_gp)

        @block.tensor
        def _(pe):
            gates_pe(pe)
            heads(pe, cell_pe)
            final_pe(pe)

        @block.scalar
        def _(act):
            gates_act(act)
            heads(act, cell_act)

        @block.vector
        def _(dve):
            gates_dve(dve)
            heads(dve, cell_dve)
            final_dve(dve)



def constants():
    headsum = np.kron(np.eye(2, dtype=np.float32), np.ones((64, 64), np.float32))
    headsel = np.zeros((NH, P), np.float32)
    for H in range(NH):
        headsel[H, 32 * (H // 4) + DECT * (H % 4):][:DECT] = 1.0
    j, t = np.arange(P)[:, None], np.arange(P)[None]
    tri = np.where(j > t, np.float32(NEG), np.float32(0))
    j, t = j[:NSM], t[:, :NSM]
    trism = np.where((j > t) | (j // DECT != t // DECT), np.float32(NEG), np.float32(0))
    blkm = (j // DECT == np.arange(DECB)[None]).astype(np.float32)
    return {"c_tri": tri, "c_trism": trism, "c_blkm": blkm, "c_headsel": headsel, "c_ident": np.eye(P, dtype=np.float32), "c_headsum": headsum, "c_onehot": diagonal_onehot()}


OUTPUTS = (
    ("y_prompt", (1, SEQ, D)),
    ("y_sample", (DECB, DECT, D)),
    ("prompt_swa_k", (1, 1, WIN, KVH, HD)),
    ("prompt_swa_v", (1, 1, WIN, KVH, HD)),
    ("prompt_swa_meta_k", (1, 1, META, KVH, HD)),
    ("prompt_swa_meta_v", (1, 1, META, KVH, HD)),
    ("prompt_mlstm_c", (1, 1, MH, MD, MD)),
    ("prompt_mlstm_n", (1, 1, MH, MD)),
    ("prompt_mlstm_m", (1, 1, MH)),
    ("prompt_conv", (1, 1, CW - 1, INNER)),
    ("sample_swa_k", (1, DECB, WIN, KVH, HD)),
    ("sample_swa_v", (1, DECB, WIN, KVH, HD)),
    ("sample_mlstm_c", (1, DECB, MH, MD, MD)),
    ("sample_mlstm_n", (1, DECB, MH, MD)),
    ("sample_mlstm_m", (1, DECB, MH)),
    ("sample_conv", (1, DECB, CW - 1, INNER)),
)


def kernel(**inputs):
    from concourse import bacc
    from concourse.bass_utils import run_bass_kernel_spmd
    arrays = {k: np.ascontiguousarray(v) for k, v in inputs.items()}
    arrays.update(constants())
    nc = bacc.Bacc("TRN2", target_bir_lowering=False, num_devices=1, dynamic_dma_scratch_size=1024)
    a = {k: nc.dram_tensor(k, v.shape, F32, kind="ExternalInput").ap() for k, v in arrays.items()}
    o = {k: nc.dram_tensor(k, s, F32, kind="ExternalOutput").ap() for k, s in OUTPUTS}
    build(nc, a, o)
    r = run_bass_kernel_spmd(nc, [arrays], core_ids=[0])
    return tuple(r.results[0][k] for k, _ in OUTPUTS)
```
